# Optimizing a Trainium2 kernel written in Bass

```python
import jax, jax.numpy as jnp
from jax import lax
import numpy as np

D_MODEL = 1024
BATCH = 1
SEQ = 256
DEPTH = 2

N_A_LAYERS = DEPTH // 2
N_B_LAYERS = DEPTH - N_A_LAYERS
LRU_WIDTH = D_MODEL
LRU_HEADS = 8
LRU_BLOCK = LRU_WIDTH // LRU_HEADS
CONV_WIDTH = 4
LRU_C = 8.0
ATTN_HEADS = 16
ATTN_HEAD_DIM = 64
ATTN_WIDTH = ATTN_HEADS * ATTN_HEAD_DIM
Q_BLOCK = 128
PEER_HEADS = 8
PEER_NKEYS = 128
PEER_EXPERTS = PEER_NKEYS * PEER_NKEYS
PEER_TOPK = 16
PEER_QDIM = 256
PEER_HALF = PEER_QDIM // 2
PEER_CHUNK = 128
PLE_DIM = 256
EPS = 1e-6


def rms_norm(x, g):
    xf = x.astype(jnp.float32)
    y = xf * lax.rsqrt(jnp.mean(xf * xf, axis=-1, keepdims=True) + EPS)
    return (y * g.astype(jnp.float32)).astype(x.dtype)

def rglru_block(h, w_in, conv_w, conv_b, w_r, w_i, b_r, b_i, lam, w_out):
    B, S, _ = h.shape
    proj = h @ w_in
    y_branch, x_branch = jnp.split(proj, 2, axis=-1)
    xc = lax.conv_general_dilated(x_branch, conv_w[:, None, :], window_strides=(1,),
                                  padding=((CONV_WIDTH - 1, 0),),
                                  dimension_numbers=('NWC', 'WIO', 'NWC'),
                                  feature_group_count=LRU_WIDTH) + conv_b
    xb = xc.reshape(B, S, LRU_HEADS, LRU_BLOCK)
    r = jax.nn.sigmoid(jnp.einsum('bshi,hij->bshj', xb, w_r).reshape(B, S, LRU_WIDTH).astype(jnp.float32)
                       + b_r.astype(jnp.float32))
    ig = jax.nn.sigmoid(jnp.einsum('bshi,hij->bshj', xb, w_i).reshape(B, S, LRU_WIDTH).astype(jnp.float32)
                        + b_i.astype(jnp.float32))
    log_a = -LRU_C * r * jax.nn.softplus(-lam.astype(jnp.float32))
    a = jnp.exp(log_a)
    u = jnp.sqrt(-jnp.expm1(2.0 * log_a)) * ig * xc.astype(jnp.float32)

    def combine(left, right):
        a1, b1 = left
        a2, b2 = right
        return a1 * a2, a2 * b1 + b2

    _, hseq = lax.associative_scan(combine, (a, u), axis=1)
    gated = (jax.nn.gelu(y_branch.astype(jnp.float32)) * hseq).astype(h.dtype)
    return gated @ w_out

def stick_breaking_attention(q, k, v):
    S = q.shape[1]
    scale = ATTN_HEAD_DIM ** -0.5
    outs = []
    for blk in range(S // Q_BLOCK):
        q0 = blk * Q_BLOCK
        end = q0 + Q_BLOCK
        qb = q[:, q0:end].astype(jnp.float32)
        kb = k[:, :end].astype(jnp.float32)
        z = jnp.einsum('bqhd,bkhd->bhqk', qb, kb) * scale
        t_pos = q0 + jnp.arange(Q_BLOCK)[:, None]
        s_pos = jnp.arange(end)[None, :]
        causal = s_pos < t_pos
        lbeta = jax.nn.log_sigmoid(z)
        l1m = jnp.where(causal, lbeta - z, 0.0)
        rc = lax.cumsum(l1m, axis=3, reverse=True)
        A = jnp.where(causal, jnp.exp(lbeta + rc - l1m), 0.0)
        outs.append(jnp.einsum('bhqk,bkhd->bqhd', A, v[:, :end].astype(jnp.float32)))
    return jnp.concatenate(outs, axis=1).astype(v.dtype)

def peer_ffn(h, w_q, sub_keys, u_tab, v_tab):
    B, S, D = h.shape
    T = B * S
    xt = h.reshape(T, D)
    q = (xt @ w_q).reshape(T, PEER_HEADS, 2, PEER_HALF).astype(jnp.float32)
    s = jnp.einsum('thpd,hpnd->thpn', q, sub_keys.astype(jnp.float32))
    sv, si = lax.top_k(s, PEER_TOPK)
    cand = sv[:, :, 0, :, None] + sv[:, :, 1, None, :]
    cv, ci = lax.top_k(cand.reshape(T, PEER_HEADS, PEER_TOPK * PEER_TOPK), PEER_TOPK)
    i1 = jnp.take_along_axis(si[:, :, 0], ci // PEER_TOPK, axis=-1)
    i2 = jnp.take_along_axis(si[:, :, 1], ci % PEER_TOPK, axis=-1)
    eidx = (i1 * PEER_NKEYS + i2).reshape(T, PEER_HEADS * PEER_TOPK)
    gates = jax.nn.softmax(cv, axis=-1).reshape(T, PEER_HEADS * PEER_TOPK)
    n_chunks = T // PEER_CHUNK

    def chunk_fn(args):
        xc, ic, gc = args
        uc = jnp.take(u_tab, ic, axis=0)
        vc = jnp.take(v_tab, ic, axis=0)
        act = jax.nn.gelu(jnp.einsum('cd,ckd->ck', xc, uc).astype(jnp.float32))
        return jnp.einsum('ck,ckd->cd', (gc * act).astype(vc.dtype), vc)

    out = lax.map(chunk_fn, (xt.reshape(n_chunks, PEER_CHUNK, D),
                             eidx.reshape(n_chunks, PEER_CHUNK, PEER_HEADS * PEER_TOPK),
                             gates.reshape(n_chunks, PEER_CHUNK, PEER_HEADS * PEER_TOPK)))
    return out.reshape(B, S, D).astype(h.dtype)

def per_layer_embed(h, p_i, g, w_gate, w_proj):
    gate = jax.nn.sigmoid((rms_norm(h, g) @ w_gate).astype(jnp.float32))
    return h + (gate * (p_i @ w_proj).astype(jnp.float32)).astype(h.dtype)

def first_inputs(seed: int = 0) -> dict:
    key = jax.random.key(seed)
    ks = jax.random.split(key, 28)
    nrm = jax.random.normal
    f32 = jnp.float32
    a8 = jax.random.uniform(ks[9], (N_A_LAYERS, LRU_WIDTH), f32, 0.9, 0.999)
    a0 = a8 ** (1.0 / LRU_C)
    return {
        'x': nrm(ks[0], (BATCH, SEQ, D_MODEL), f32),
        'p': nrm(ks[1], (DEPTH, BATCH, SEQ, PLE_DIM), f32),
        'norm_mix': 1.0 + 0.02 * nrm(ks[2], (DEPTH, D_MODEL), f32),
        'a_w_in': nrm(ks[3], (N_A_LAYERS, D_MODEL, 2 * LRU_WIDTH), f32) * D_MODEL ** -0.5,
        'a_conv_w': nrm(ks[4], (N_A_LAYERS, CONV_WIDTH, LRU_WIDTH), f32) * CONV_WIDTH ** -0.5,
        'a_conv_b': 0.02 * nrm(ks[5], (N_A_LAYERS, LRU_WIDTH), f32),
        'a_w_r': nrm(ks[6], (N_A_LAYERS, LRU_HEADS, LRU_BLOCK, LRU_BLOCK), f32) * LRU_BLOCK ** -0.5,
        'a_w_i': nrm(ks[7], (N_A_LAYERS, LRU_HEADS, LRU_BLOCK, LRU_BLOCK), f32) * LRU_BLOCK ** -0.5,
        'a_b_r': 0.02 * nrm(ks[8], (N_A_LAYERS, LRU_WIDTH), f32),
        'a_b_i': 0.02 * nrm(ks[10], (N_A_LAYERS, LRU_WIDTH), f32),
        'a_lambda': jnp.log(a0) - jnp.log1p(-a0),
        'a_w_out': nrm(ks[11], (N_A_LAYERS, LRU_WIDTH, D_MODEL), f32) * LRU_WIDTH ** -0.5,
        'kv_norm': 1.0 + 0.02 * nrm(ks[12], (D_MODEL,), f32),
        'w_kv': nrm(ks[13], (D_MODEL, 2 * ATTN_WIDTH), f32) * D_MODEL ** -0.5,
        'b_w_q': nrm(ks[14], (N_B_LAYERS, D_MODEL, ATTN_WIDTH), f32) * D_MODEL ** -0.5,
        'b_w_o': nrm(ks[15], (N_B_LAYERS, ATTN_WIDTH, D_MODEL), f32) * ATTN_WIDTH ** -0.5,
        'norm_ffn': 1.0 + 0.02 * nrm(ks[16], (DEPTH, D_MODEL), f32),
        'peer_w_q': nrm(ks[17], (DEPTH, D_MODEL, PEER_HEADS * PEER_QDIM), f32) * D_MODEL ** -0.5,
        'peer_sub_keys': nrm(ks[18], (DEPTH, PEER_HEADS, 2, PEER_NKEYS, PEER_HALF), f32) * PEER_HALF ** -0.5,
        'peer_u': nrm(ks[19], (DEPTH, PEER_EXPERTS, D_MODEL), f32) * D_MODEL ** -0.5,
        'peer_v': nrm(ks[20], (DEPTH, PEER_EXPERTS, D_MODEL), f32) * (PEER_HEADS * PEER_TOPK) ** -0.5,
        'norm_ple': 1.0 + 0.02 * nrm(ks[21], (DEPTH, D_MODEL), f32),
        'ple_w_gate': nrm(ks[22], (DEPTH, D_MODEL, D_MODEL), f32) * D_MODEL ** -0.5,
        'ple_w_proj': nrm(ks[23], (DEPTH, PLE_DIM, D_MODEL), f32) * PLE_DIM ** -0.5,
        'final_norm': 1.0 + 0.02 * nrm(ks[24], (D_MODEL,), f32),
    }

def first_block(x, p, norm_mix, a_w_in, a_conv_w, a_conv_b, a_w_r, a_w_i, a_b_r, a_b_i, a_lambda,
              a_w_out, kv_norm, w_kv, b_w_q, b_w_o, norm_ffn, peer_w_q, peer_sub_keys, peer_u,
              peer_v, norm_ple, ple_w_gate, ple_w_proj, final_norm):
    B, S, _ = x.shape
    h = x
    k_shared = None
    v_shared = None
    for i in range(DEPTH):
        hn = rms_norm(h, norm_mix[i])
        if i < N_A_LAYERS:
            j = i
            h = h + rglru_block(hn, a_w_in[j], a_conv_w[j], a_conv_b[j], a_w_r[j], a_w_i[j],
                                a_b_r[j], a_b_i[j], a_lambda[j], a_w_out[j])
        else:
            j = i - N_A_LAYERS
            if i == N_A_LAYERS:
                kvp = rms_norm(h, kv_norm) @ w_kv
                k_flat, v_flat = jnp.split(kvp, 2, axis=-1)
                k_shared = k_flat.reshape(B, S, ATTN_HEADS, ATTN_HEAD_DIM)
                v_shared = v_flat.reshape(B, S, ATTN_HEADS, ATTN_HEAD_DIM)
            q = (hn @ b_w_q[j]).reshape(B, S, ATTN_HEADS, ATTN_HEAD_DIM)
            o = stick_breaking_attention(q, k_shared, v_shared).reshape(B, S, ATTN_WIDTH)
            h = h + o @ b_w_o[j]
        h = h + peer_ffn(rms_norm(h, norm_ffn[i]), peer_w_q[i], peer_sub_keys[i], peer_u[i], peer_v[i])
        h = per_layer_embed(h, p[i], norm_ple[i], ple_w_gate[i], ple_w_proj[i])
    return rms_norm(h, final_norm)


DEPTH_2 = 1

D_ATTN = D_MODEL // 2
HEAD_DIM_A = 64
N_HEADS_A = D_ATTN // HEAD_DIM_A
DILATED_PAIRS = ((128, 1), (512, 4), (2048, 16))
D_REC = D_MODEL - D_ATTN
HGRN_EXPAND = 128
N_HEADS_R = D_REC // HGRN_EXPAND
HEAD_DIM_R = D_REC // N_HEADS_R
HGRN_CHUNK = 32
D_FORGET = N_HEADS_R * HGRN_EXPAND
D_IN = 3 * D_ATTN + 2 * D_FORGET + 2 * D_REC
N_EXPERTS = 32
TOP_K = 4
D_FF = D_MODEL
SWIGLU_LIMIT = 7.0
SWIGLU_ALPHA = 1.702
MOE_BLOCK = 128


def rms_norm_2(x, w):
    xf = x.astype(jnp.float32)
    y = xf * lax.rsqrt(jnp.mean(xf * xf, axis=-1, keepdims=True) + EPS)
    return (y * w.astype(jnp.float32)).astype(x.dtype)

def modulate(n, shift, scale):
    return n * (1.0 + scale[:, None, :]) + shift[:, None, :]

def dilated_causal_attention(q, k, v, window, dil):
    B, S, H, Dh = q.shape
    bw = window // dil
    n = S // dil
    nb = -(-n // bw)
    pad = nb * bw - n

    def sub(t):
        t = t.reshape(B, n, dil, H, Dh).transpose(0, 2, 1, 3, 4)
        return jnp.pad(t, ((0, 0), (0, 0), (0, pad), (0, 0), (0, 0)))

    def band(t):
        tp = jnp.pad(t, ((0, 0), (0, 0), (bw, 0), (0, 0), (0, 0)))
        prev = tp[:, :, :nb * bw].reshape(B, dil, nb, bw, H, Dh)
        cur = t.reshape(B, dil, nb, bw, H, Dh)
        return jnp.concatenate([prev, cur], axis=3)

    qb = sub(q).reshape(B, dil, nb, bw, H, Dh).astype(jnp.float32)
    kb = band(sub(k)).astype(jnp.float32)
    vb = band(sub(v)).astype(jnp.float32)

    r = jnp.arange(bw)[:, None]
    j = jnp.arange(2 * bw)[None, :]
    diff = bw + r - j
    kidx = (jnp.arange(nb)[:, None, None] - 1) * bw + j[None]
    mask = (diff >= 0) & (diff <= bw) & (kidx >= 0)

    s = jnp.einsum('bgiqhd,bgikhd->bgihqk', qb, kb) * (Dh ** -0.5)
    s = jnp.where(mask[None, None, :, None], s, -jnp.inf)
    m = jnp.max(s, axis=-1, keepdims=True)
    p = jnp.exp(s - m)
    l = jnp.sum(p, axis=-1, keepdims=True)
    o = jnp.einsum('bgihqk,bgikhd->bgiqhd', p, vb) / jnp.swapaxes(l, 3, 4)
    lse = jnp.swapaxes((m + jnp.log(l))[..., 0], 3, 4)

    o = o.reshape(B, dil, nb * bw, H, Dh)[:, :, :n].transpose(0, 2, 1, 3, 4).reshape(B, S, H, Dh)
    lse = lse.reshape(B, dil, nb * bw, H)[:, :, :n].transpose(0, 2, 1, 3).reshape(B, S, H)
    return o, lse

def hgrn2_chunkwise(q, k, v, log_f):
    B, S, H, DK = q.shape
    DV = v.shape[-1]
    C = HGRN_CHUNK
    nc = S // C

    def chunk(t):
        return t.astype(jnp.float32).reshape(B, nc, C, H, t.shape[-1]).transpose(0, 3, 1, 2, 4)

    q, k, v, log_f = chunk(q), chunk(k), chunk(v), chunk(log_f)
    b = jnp.cumsum(log_f, axis=3)
    qe = q * jnp.exp(b)
    ke = k * jnp.exp(-b)
    causal = jnp.tril(jnp.ones((C, C), dtype=bool))
    a = jnp.where(causal, jnp.einsum('bhncd,bhnsd->bhncs', qe, ke), 0.0)
    o_intra = jnp.einsum('bhncs,bhnse->bhnce', a, v)

    b_last = b[:, :, :, -1:, :]
    delta = jnp.einsum('bhncd,bhnce->bhnde', k * jnp.exp(b_last - b), v)
    decay = jnp.exp(b_last[:, :, :, 0, :])

    def step(state, inp):
        dec, dl = inp
        return dec[..., None] * state + dl, state

    s0 = jnp.zeros((B, H, DK, DV), jnp.float32)
    _, s_prev = lax.scan(step, s0, (jnp.moveaxis(decay, 2, 0), jnp.moveaxis(delta, 2, 0)))
    s_prev = jnp.moveaxis(s_prev, 0, 2)
    o_inter = jnp.einsum('bhncd,bhnde->bhnce', qe, s_prev)
    return (o_intra + o_inter).transpose(0, 2, 3, 1, 4).reshape(B, S, H, DV)

def hybrid_mixer(h, w_in, attn_norm_w, lb, hgrn_norm_w, w_out):
    B, S, _ = h.shape
    proj = h @ w_in
    widths = [D_ATTN, D_ATTN, D_ATTN, D_FORGET, D_FORGET, D_REC, D_REC]
    cuts = [int(v) for v in np.cumsum(widths)[:-1]]
    qa, ka, va, qr, fr, ir, gr = jnp.split(proj, cuts, axis=-1)

    qa = qa.reshape(B, S, N_HEADS_A, HEAD_DIM_A)
    ka = ka.reshape(B, S, N_HEADS_A, HEAD_DIM_A)
    va = va.reshape(B, S, N_HEADS_A, HEAD_DIM_A)
    outs, lses = [], []
    for window, dil in DILATED_PAIRS:
        o, lse = dilated_causal_attention(qa, ka, va, window, dil)
        outs.append(o)
        lses.append(lse)
    wts = jax.nn.softmax(jnp.stack(lses, axis=0), axis=0)
    o_a = jnp.einsum('nbsh,nbshd->bshd', wts, jnp.stack(outs, axis=0)).astype(h.dtype)
    y_a = rms_norm_2(o_a, attn_norm_w.reshape(N_HEADS_A, HEAD_DIM_A)).reshape(B, S, D_ATTN)

    q_r = jax.nn.silu(qr.astype(jnp.float32)).reshape(B, S, N_HEADS_R, HGRN_EXPAND)
    lb_h = lb.reshape(N_HEADS_R, HGRN_EXPAND)
    f = lb_h + (1.0 - lb_h) * jax.nn.sigmoid(fr.astype(jnp.float32).reshape(B, S, N_HEADS_R, HGRN_EXPAND))
    v_r = ir.reshape(B, S, N_HEADS_R, HEAD_DIM_R)
    o_r = hgrn2_chunkwise(q_r, 1.0 - f, v_r, jnp.log(f)).astype(h.dtype)
    o_r = rms_norm_2(o_r, hgrn_norm_w.reshape(N_HEADS_R, HEAD_DIM_R)).reshape(B, S, D_REC)
    y_r = o_r * jax.nn.silu(gr)

    return jnp.concatenate([y_a, y_r], axis=-1) @ w_out

def moe_ffn(h, w_router, b_router, w_gu, b_gu, w_down, b_down):
    B, S, D = h.shape
    T = B * S
    ht = h.reshape(T, D)
    logits = (ht @ w_router + b_router).astype(jnp.float32)
    top_val, top_idx = lax.top_k(logits, TOP_K)
    gates = jax.nn.softmax(top_val, axis=-1)

    flat_e = top_idx.reshape(-1)
    flat_tok = jnp.arange(T * TOP_K, dtype=jnp.int32) // TOP_K
    flat_gate = gates.reshape(-1)
    order = jnp.argsort(flat_e)
    se, stok, sgate = flat_e[order], flat_tok[order], flat_gate[order]
    counts = jnp.zeros((N_EXPERTS,), jnp.int32).at[flat_e].add(1)
    padded = ((counts + MOE_BLOCK - 1) // MOE_BLOCK) * MOE_BLOCK
    pend = jnp.cumsum(padded)
    pstart = pend - padded
    sstart = jnp.cumsum(counts) - counts
    rank = jnp.arange(T * TOP_K, dtype=jnp.int32) - sstart[se]
    dest = pstart[se] + rank
    P = T * TOP_K + N_EXPERTS * MOE_BLOCK
    nblk = P // MOE_BLOCK
    tok_pad = jnp.full((P,), T, jnp.int32).at[dest].set(stok)
    gate_pad = jnp.zeros((P,), h.dtype).at[dest].set(sgate.astype(h.dtype))
    blk_e = jnp.minimum(jnp.searchsorted(pend, jnp.arange(nblk) * MOE_BLOCK, side='right'),
                        N_EXPERTS - 1).astype(jnp.int32)
    x_pad = jnp.concatenate([ht, jnp.zeros((1, D), ht.dtype)], axis=0)
    xb = x_pad[tok_pad].reshape(nblk, MOE_BLOCK, D)

    def expert_block(args):
        xblk, e = args
        hg = xblk @ w_gu[e] + b_gu[e]
        x_glu, x_lin = hg[:, :D_FF], hg[:, D_FF:]
        x_glu = jnp.minimum(x_glu, SWIGLU_LIMIT)
        x_lin = jnp.clip(x_lin, -SWIGLU_LIMIT, SWIGLU_LIMIT)
        act = x_glu * jax.nn.sigmoid(SWIGLU_ALPHA * x_glu) * (x_lin + 1.0)
        return act @ w_down[e] + b_down[e]

    yb = lax.map(expert_block, (xb, blk_e))
    y = yb.reshape(P, D) * gate_pad[:, None]
    out = jnp.zeros((T + 1, D), y.dtype).at[tok_pad].add(y)[:T]
    return out.reshape(B, S, D)

def second_inputs(seed: int = 0) -> dict:
    key = jax.random.key(seed)
    ks = jax.random.split(key, 20)

    def nrm(k, shape, scale):
        return jax.random.normal(k, shape, jnp.float32) * scale

    return {
        "x": nrm(ks[0], (BATCH, SEQ, D_MODEL), 1.0),
        "c": nrm(ks[1], (BATCH, D_MODEL), 1.0),
        "w_ada": nrm(ks[2], (DEPTH_2, D_MODEL, 6 * D_MODEL), 0.5 * D_MODEL ** -0.5),
        "b_ada": nrm(ks[3], (DEPTH_2, 6 * D_MODEL), 0.02),
        "g_pre_mix": 1.0 + nrm(ks[4], (DEPTH_2, D_MODEL), 0.05),
        "g_post_mix": 1.0 + nrm(ks[5], (DEPTH_2, D_MODEL), 0.05),
        "w_in": nrm(ks[6], (DEPTH_2, D_MODEL, D_IN), D_MODEL ** -0.5),
        "attn_norm_w": 1.0 + nrm(ks[7], (DEPTH_2, D_ATTN), 0.05),
        "hgrn_lb": nrm(ks[8], (DEPTH_2 + 1, D_FORGET), 0.5),
        "hgrn_norm_w": 1.0 + nrm(ks[9], (DEPTH_2, D_REC), 0.05),
        "w_out": nrm(ks[10], (DEPTH_2, D_MODEL, D_MODEL), D_MODEL ** -0.5),
        "g_pre_ffn": 1.0 + nrm(ks[11], (DEPTH_2, D_MODEL), 0.05),
        "g_post_ffn": 1.0 + nrm(ks[12], (DEPTH_2, D_MODEL), 0.05),
        "w_router": nrm(ks[13], (DEPTH_2, D_MODEL, N_EXPERTS), D_MODEL ** -0.5),
        "b_router": nrm(ks[14], (DEPTH_2, N_EXPERTS), 0.01),
        "w_gu": nrm(ks[15], (DEPTH_2, N_EXPERTS, D_MODEL, 2 * D_FF), D_MODEL ** -0.5),
        "b_gu": nrm(ks[16], (DEPTH_2, N_EXPERTS, 2 * D_FF), 0.02),
        "w_down": nrm(ks[17], (DEPTH_2, N_EXPERTS, D_FF, D_MODEL), D_FF ** -0.5),
        "b_down": nrm(ks[18], (DEPTH_2, N_EXPERTS, D_MODEL), 0.02),
    }

def second_block(x, c, w_ada, b_ada, g_pre_mix, g_post_mix, w_in, attn_norm_w, hgrn_lb,
              hgrn_norm_w, w_out, g_pre_ffn, g_post_ffn, w_router, b_router, w_gu, b_gu,
              w_down, b_down):
    lb_table = jnp.cumsum(jax.nn.softmax(hgrn_lb.astype(jnp.float32), axis=0), axis=0)
    cond = jax.nn.silu(c)
    for l in range(DEPTH_2):
        mod = cond @ w_ada[l] + b_ada[l]
        shift_m, scale_m, gate_m, shift_f, scale_f, gate_f = jnp.split(mod, 6, axis=-1)
        h = modulate(rms_norm_2(x, g_pre_mix[l]), shift_m, scale_m)
        y = hybrid_mixer(h, w_in[l], attn_norm_w[l], lb_table[l], hgrn_norm_w[l], w_out[l])
        x = x + gate_m[:, None, :] * rms_norm_2(y, g_post_mix[l])
        h = modulate(rms_norm_2(x, g_pre_ffn[l]), shift_f, scale_f)
        y = moe_ffn(h, w_router[l], b_router[l], w_gu[l], b_gu[l], w_down[l], b_down[l])
        x = x + gate_f[:, None, :] * rms_norm_2(y, g_post_ffn[l])
    return x


def setup_inputs(seed=0):
    out = dict(first_inputs(seed))
    for name, value in second_inputs(seed + 1).items():
        if name != "x":
            out[name + "_2"] = value
    return out


def reference(
    x, p, norm_mix, a_w_in, a_conv_w, a_conv_b, a_w_r, a_w_i, a_b_r, a_b_i, a_lambda, a_w_out,
    kv_norm, w_kv, b_w_q, b_w_o, norm_ffn, peer_w_q, peer_sub_keys, peer_u, peer_v, norm_ple,
    ple_w_gate, ple_w_proj, final_norm, c_2, w_ada_2, b_ada_2, g_pre_mix_2, g_post_mix_2,
    w_in_2, attn_norm_w_2, hgrn_lb_2, hgrn_norm_w_2, w_out_2, g_pre_ffn_2, g_post_ffn_2,
    w_router_2, b_router_2, w_gu_2, b_gu_2, w_down_2, b_down_2,
):
    x = first_block(
        x, p, norm_mix, a_w_in, a_conv_w, a_conv_b, a_w_r, a_w_i, a_b_r, a_b_i, a_lambda,
        a_w_out, kv_norm, w_kv, b_w_q, b_w_o, norm_ffn, peer_w_q, peer_sub_keys, peer_u, peer_v,
        norm_ple, ple_w_gate, ple_w_proj, final_norm,
    )
    return second_block(
        x, c_2, w_ada_2, b_ada_2, g_pre_mix_2, g_post_mix_2, w_in_2, attn_norm_w_2, hgrn_lb_2,
        hgrn_norm_w_2, w_out_2, g_pre_ffn_2, g_post_ffn_2, w_router_2, b_router_2, w_gu_2,
        b_gu_2, w_down_2, b_down_2,
    )


_drawn_inputs = setup_inputs


def setup_inputs(seed=0):
    import zlib

    import numpy as np

    out = dict(_drawn_inputs(seed))
    spreads = {}
    factors = {'a_b_r': 5.425,
     'a_b_i': 5.209,
     'norm_ffn': 2.799,
     'norm_ple': 4.641,
     'hgrn_lb_2': 3.028,
     'hgrn_norm_w_2': 2.674,
     'g_post_ffn_2': 3.97,
     'b_router_2': 2.669,
     'b_gu_2': 8.0,
     'b_down_2': 8.0}
    for name, (base, spread) in spreads.items():
        noise = np.random.default_rng([zlib.crc32(name.encode()), seed]).standard_normal(out[name].shape)
        drawn = base * np.exp(spread * noise) if base else spread * noise
        out[name] = __import__('jax').numpy.asarray(drawn.astype(out[name].dtype))
    for name, factor in factors.items():
        out[name] = (out[name] * factor).astype(out[name].dtype)
    return out
```

```python
from contextlib import ExitStack

import numpy as np
import concourse.bass as bass
from concourse import mybir

F32 = mybir.dt.float32
U32 = mybir.dt.uint32
I32 = mybir.dt.int32
ALU = mybir.AluOpType
ACT = mybir.ActivationFunctionType
AX = mybir.AxisListType

P = 128
T = 256
TT = T // P
D = 1024
KC = D // P
EPS = 1e-6
HEADS = 16
PH = 8
NK = 128
TOPK = 16
E2 = 32
DIL_HEADS = 8
REC_HEADS = 4
CHUNK = 32
RING = 3
SLOT = 4096
NEG = -3.0e38
SC = 0.125

STREAM = (
    ("a_in", 4, "AA"), ("a_gates", 1, "A" * 8), ("a_out", 2, "DD"),
    ("peer_q0", 4, "AA"), ("peer_keys0", 1, "A" * 8), ("peer_u0", 32, "AA"), ("peer_v0", 32, "--"),
    ("ple_gate0", 2, "AA"), ("ple_proj0", 1, "DDDD"),
    ("kv", 4, "AA"), ("bq", 2, "AA"), ("bo", 2, "DD"),
    ("peer_q1", 4, "AA"), ("peer_keys1", 1, "A" * 8), ("peer_u1", 32, "AA"), ("peer_v1", 32, "--"),
    ("ple_gate1", 2, "AA"), ("ple_proj1", 1, "DDDD"),
    ("ada", 12, "DD"), ("mix_in", 7, ("AA", "AA", "AA", "DD", "AA", "AA", "DD")), ("mix_out", 2, "DD"),
    ("moe", 6, ("D", "D", "D", "DAAA", "A", "A")),
)
BLOCK_TILES = 9


def stream_plan():
    first, ends, engine, nth = {}, [], [], []
    count = {"A": 0, "D": 0, "-": 0}
    for stage, slots, who in STREAM:
        first[stage] = len(ends)
        for s in range(slots):
            for e in (who[s] if isinstance(who, tuple) else who):
                count[e] += 1
                engine.append(e)
                nth.append(count[e])
            ends.append(len(engine))
    return first, ends, engine, nth


VECS = ("norm_mix0", "norm_mix1", "kv_norm", "norm_ffn0", "norm_ffn1", "norm_ple0", "norm_ple1", "final_norm",
        "conv0", "conv1", "conv2", "conv3", "conv_b", "b_r", "b_i", "lam",
        "g_pre_mix", "g_post_mix", "g_pre_ffn", "g_post_ffn", "mix_norm", "c", "lb",
        "ada0", "ada1", "ada2", "ada3", "ada4", "ada5")
V = {n: i for i, n in enumerate(VECS)}

C_MASK, C_TRI, C_ONES, C_NEG, C_CNT, C_REC, C_RESET = 0, 384, 512, 640, 1024, 1408, 1536
C_IOTA32, C_END = 1792, 1824


def constant_tables():
    k = np.arange(P)[:, None]
    q = np.arange(P)[None, :]
    one = np.ones((P, P), np.float32)
    strict = (k < q).astype(np.float32)
    mask = np.concatenate([strict, one, strict], 1)
    tri = (k > q).astype(np.float32)
    def count(q0, k0):
        d = (q0 + k) - (k0 + q)
        n = ((d >= 0) & (d <= 128)).astype(np.float32)
        n += ((d >= 0) & (d % 4 == 0) & (d <= 512))
        n += ((d >= 0) & (d % 16 == 0) & (d <= 2048))
        return n.astype(np.float32)
    cnt = np.concatenate([count(0, 0), count(128, 0), count(128, 128)], 1)
    neg = np.where(cnt > 0, 0.0, -1e30).astype(np.float32)
    rec = ((k // CHUNK == q // CHUNK) & (k <= q)).astype(np.float32)
    reset = np.tile((np.arange(T) % CHUNK != 0).astype(np.float32), (P, 1))
    iota = np.tile(np.arange(32, dtype=np.float32), (P, 1))
    small = np.concatenate([np.eye(P, dtype=np.float32), np.tile(np.arange(P, dtype=np.float32), (P, 1))], 1)
    late = np.concatenate([mask, tri, one, neg, cnt, rec, reset, iota], 1)
    assert late.shape[1] == C_END
    return small, late


def build(nc, d):
    FIRST, ENDS, TILE_ENGINE, TILE_NTH = stream_plan()

    def tile0(stage):
        s = FIRST[stage]
        return ENDS[s - 1] if s else 0

    with ExitStack() as ctx:
        def sb(name, shape, dt=F32):
            return ctx.enter_context(nc.sbuf_tensor(name, shape, dt))

        def sem(name):
            return ctx.enter_context(nc.semaphore(name))

        ring = sb("ring", [P, RING, SLOT])
        big = sb("big", [P, 32768])
        h = sb("h", [P, TT, D])
        xT = sb("xT", [P, KC, T])
        small = sb("small", [P, 2 * P])
        ident = small[:, 0:P]
        iota = small[:, P:2 * P]
        vecs = sb("vecs", [P, len(VECS), 8])
        ss = sb("ss", [P, 2])
        ms = sb("ms", [P, 2])
        std = sb("std", [P, 2])
        rstd = sb("rstd", [P, 2])
        pick = sb("pick", [P, 3, TT, P])
        pickT = sb("pickT", [P, 3, T])
        cval = sb("cval", [P, TT, PH, TOPK])
        sv = sb("sv", [P, 2, TOPK])
        si = sb("si", [P, 2, TOPK], U32)
        sif = sb("sif", [P, 2, TOPK])
        keys_in = sb("keys_in", [P, 2, NK])
        work = sb("work", [P, TOPK, TOPK])
        cand = sb("cand", [P, TOPK, TOPK])
        cv = sb("cv", [P, TOPK])
        ci = sb("ci", [P, TOPK], U32)
        cab = sb("cab", [P, 2, TOPK], U32)
        cabf = sb("cabf", [P, 2, TOPK])
        tiny = sb("tiny", [P, 16, 8])
        psum = ctx.enter_context(nc.psum_tensor("psum", [P, 8, 512], F32))

        def V8(name):
            return vecs[:, V[name], :]

        def region(at, *shape):
            n = int(np.prod(shape))
            v = big[:, at:at + n]
            if len(shape) == 2:
                return v.rearrange("p (a b) -> p a b", a=shape[0])
            if len(shape) == 3:
                return v.rearrange("p (a b c) -> p a b c", a=shape[0], b=shape[1])
            return v

        hs = region(0, TT, D)

        acts = region(0, NK, T)
        scores = region(112 * T, TT, 16, NK)
        qT = region(96 * T, 16, T)
        xflat = xT[:].rearrange("p a b -> p (a b)")
        hot = xflat.rearrange("p (b r k n) -> p b r k n", b=2, r=2, k=4)
        vstage = xflat.rearrange("p (b c) -> p b c", b=2)

        gy = region(2048, KC, T)
        xb = region(4096, KC, T + 3)
        xc = region(4096 + KC * (T + 3), KC, T)
        lru = [region(8448 + 2048 * i, KC, T) for i in range(6)]

        gate_sb = region(2048, TT, D)
        ple_t = region(4096, TT, D)
        pT = region(6144, 2, T)

        xT2 = region(2048, KC, T)
        kT = region(4096, KC, T)
        qbT = region(6144, KC, T)
        v_sb = region(8192, TT, D)
        oT = region(10240, KC, T)
        late = region(12288, C_END)
        w_sb = region(14336, HEADS, 384)
        lm = region(20480, HEADS, 384)
        za = region(26624, 3, 2, 384)
        zl = region(28928, 2, 384)

        row = region(2048, D)
        diag = region(3072, KC, P)
        modv = sb("modv", [P, 48])
        qaT = region(4096, 4, T)
        kaT = region(5120, 4, T)
        va = region(6144, TT, 512)
        qrT = region(7168, 4, T)
        frT = region(8192, 4, T)
        vr = region(9216, TT, 512)
        gr = region(10240, TT, 512)
        ylow = region(16384, TT, D)
        sm = region(18432, 2, 384)
        em = region(19200, 2, 384)
        pmT = region(19968, 2, 384)
        dnum = region(20736, 8, 4)
        sq = region(20768, TT, D)
        hst = region(22816, 24)
        f_ = region(24576, 4, T)
        b_ = region(25600, 4, T)
        eb = region(26624, 4, T)
        qe = region(27648, 4, T)
        ke = region(28672, 4, T)
        kd = region(29696, 4, T)
        kdt = region(30720, 4, TT, P)
        am = region(22912, 4, TT, P)
        states = region(14336, 4, 4, P)
        blast = region(31744, 4, 8)
        decay = region(31776, 4, 8)
        ysb = region(18432, TT, D)

        bgu = region(4096, 2 * E2, 16)
        bdn = region(5120, D)
        wr = region(6144, KC, E2)
        br = region(6400, E2)
        rank = region(6464, TT, 66)
        G2 = region(6600, TT, 66)
        member = region(6740, TT, E2)
        G = region(6820, TT, E2)
        logit = region(6890, TT, E2)
        gT = region(6960, T)
        tk = region(7220, 64)
        tki = region(7290, 16).bitcast(U32)
        most = region(7310, E2)
        blocks = region(7350, 1).bitcast(I32)
        actT = region(8192, KC, P)
        xgT = region(9216, KC, P)
        S = region(10240, TT, P)
        SG = region(10496, TT, P)
        SGT = region(10752, T)
        Y = region(11008, D)
        xg = region(14336, 2, 2, P)
        sgm = region(14848, 2, 2, P)
        lin = region(15360, 2, 2, P)
        row2 = region(16384, D)
        acc = region(18432, TT, D)

        loaded = [sem(f"slot_loaded{i}") for i in range(RING)]
        tile_done = sem("tile_done")
        act_took = sem("act_took")
        dve_took = sem("dve_took")
        x_loaded = sem("x_loaded")
        small_loaded = sem("small_loaded")
        var_ready, std_ready, hs_ready = sem("var_ready"), sem("std_ready"), sem("hs_ready")
        turned, xT_ready = sem("turned"), sem("xT_ready")
        pads_ready, conv_ready, spl_ready = sem("pads_ready"), sem("conv_ready"), sem("spl_ready")
        expl_ready = sem("expl_ready")
        tanh_ready, sqrt_ready, gated_ready = sem("tanh_ready"), sem("sqrt_ready"), sem("gated_ready")
        topk_done, gexp_in, gexp_out = sem("topk_done"), sem("gexp_in"), sem("gexp_out")
        pick_ready, pick_turned, pickT_ready = sem("pick_ready"), sem("pick_turned"), sem("pickT_ready")
        hot_ready, wmat_done, gated_acts = sem("hot_ready"), sem("wmat_done"), sem("gated_acts")
        vstage_ready, residual_ready = sem("vstage_ready"), sem("residual_ready")
        p_loaded, late_loaded = sem("p_loaded"), sem("late_loaded")
        z_done, zabs_ready, zlog_ready, lm_ready = sem("z_done"), sem("zabs_ready"), sem("zlog_ready"), sem("lm_ready")
        suffix_done, aexp_in, aexp_out, a_ready = sem("suffix_done"), sem("aexp_in"), sem("aexp_out"), sem("a_ready")
        o_done, o_taken = sem("o_done"), sem("o_taken")
        cond_sig, cond_ready, diag_ready, row_done, row_taken = (
            sem("cond_sig"), sem("cond_ready"), sem("diag_ready"), sem("row_done"), sem("row_taken"))
        silu_sig, silu_taken = sem("silu_sig"), sem("silu_taken")
        da_done, da_in, da_exp, da_p, da_turned, da_copied, da_o, da_taken = [sem(f"dil_{n}") for n in (
            "scores", "max", "exp", "probs", "turned", "copied", "out", "taken")]
        lb_in, lb_sig, f_ready, logf_ready, b_ready, eb_ready, kd_ready = [sem(f"rec_{n}") for n in (
            "lb_in", "lb_sig", "f", "logf", "b", "exp", "kd")]
        kdt_done, kdt_taken, am_done, am_taken, delta_done, state_ready, ro_done = [sem(f"rec_{n}") for n in (
            "kdt_done", "kdt_taken", "am_done", "am_taken", "delta_done", "state", "out")]
        moe_loaded, logits_done, gexp2_in, gexp2_out, g_ready, gT_done, gT_ready, bd_done, act_ready, sig_ready = [
            sem(f"moe_{n}") for n in ("loaded", "logits", "exp_in", "exp_out", "gates", "gates_turned", "gatesT",
                                      "bias_out", "act", "sigmoid")]
        blocks_ready, first_S, gather0_done, gather0_taken, S_ready, moe_done = [sem(f"moe_{n}") for n in (
            "blocks", "first_onehot", "gather0_done", "gather0_taken", "onehot", "done")]
        member_ready, ranks_done = sem("moe_member"), sem("moe_ranks")
        y_ready, out_stored = sem("y_ready"), sem("out_stored")

        block = ctx.enter_context(nc.Block())

        @block.sync
        def _(sp):
            sp.dma_start(h[:], d["x"][0].rearrange("(a p) d -> p a d", p=P)).then_inc(x_loaded, 16)

            def load(n, src, words=SLOT, free_at=None):
                if n >= RING:
                    sp.wait_ge(tile_done, ENDS[n - RING] if free_at is None else free_at)
                sp.dma_start(ring[:, n % RING, 0:words], src).then_inc(loaded[n % RING], 16)

            def plain(stage, w):
                for s in range(w.shape[0]):
                    load(FIRST[stage] + s, w[s])

            def long(stage, w, slots, body):
                n0 = FIRST[stage]
                for s in range(RING):
                    load(n0 + s, w[s])
                rolled = (slots - RING) // body * body
                with sp.Fori(0, rolled // body) as i:
                    for j in range(body):
                        load(n0 + RING + j, w[i * body + (RING + j)], free_at=i * (2 * body) + ENDS[n0 + j])
                for s in range(RING + rolled, slots):
                    load(n0 + s, w[s])

            def peer(l):
                plain(f"peer_q{l}", d["peer_wq"][l])
                load(FIRST[f"peer_keys{l}"], d["keys"][l], words=16 * NK)
                long(f"peer_u{l}", d["peer_u"][l], 32, RING)
                long(f"peer_v{l}", d["peer_v"][l], 32, RING)
                plain(f"ple_gate{l}", d["ple_gate"][l])
                load(FIRST[f"ple_proj{l}"], d["ple_proj"][l], words=2 * D)

            plain("a_in", d["a_in"])
            load(FIRST["a_gates"], d["a_gates"], words=16 * P)
            plain("a_out", d["a_out"])
            peer(0)
            plain("kv", d["kv"])
            plain("bq", d["bq"])
            plain("bo", d["bo"])
            peer(1)
            plain("ada", d["ada"])
            plain("mix_in", d["mix_in"])
            plain("mix_out", d["mix_out"])
            n0 = FIRST["moe"]
            w = d["moe"]
            for s in range(RING):
                load(n0 + s, w[0, s])
            sp.wait_ge(blocks_ready, 1)
            n = sp.value_load(blocks[0:1, 0:1], min_val=E2, max_val=2 * E2)
            with sp.Fori(0, n - 1) as i:
                for s in range(RING):
                    load(n0 + RING + s, w[i % E2, RING + s], free_at=i * BLOCK_TILES + ENDS[n0 + s])
                for s in range(RING):
                    load(n0 + 2 * RING + s, w[(i + 1) % E2, s], free_at=i * BLOCK_TILES + ENDS[n0 + RING + s])
            for s in range(RING):
                load(n0 + RING + s, w[E2 - 1, RING + s], free_at=(n - 1) * BLOCK_TILES + ENDS[n0 + s])
            sp.wait_ge(y_ready, TT)
            sp.dma_start(d["out"][0].rearrange("(a p) d -> p a d", p=P), hs).then_inc(out_stored, 16)
            sp.wait_ge(out_stored, 16)

        @block.tensor
        def _(pe):
            def slot_in(n, extra=0):
                pe.wait_ge(loaded[n % RING], extra + 16 * (n // RING + 1))
                return ring[:, n % RING, :]

            def bank_free(m):
                if m >= 3 and TILE_ENGINE[m - 3] != "-":
                    pe.wait_ge(act_took if TILE_ENGINE[m - 3] == "A" else dve_took, TILE_NTH[m - 3])

            def features(stage, s, rhs, free=bank_free, extra=0, n=None):
                n = FIRST[stage] + s if n is None else n
                w = slot_in(n, extra).rearrange("p (k f) -> p k f", k=KC)
                m = ENDS[n] - 2
                for t in range(2):
                    free(m + t)
                    for f in range(2):
                        c = (2 * t + f) * P
                        for k in range(KC):
                            mm = pe.matmul(psum[:, (m + t) % 3, f * T:(f + 1) * T], w[:, k, c:c + P], rhs[:, k, :],
                                           start=(k == 0), stop=(k == KC - 1))
                    mm.then_inc(tile_done, 1)

            def tokens(stage, s, lhs, free=bank_free, extra=0, n=None):
                n = FIRST[stage] + s if n is None else n
                w = slot_in(n, extra).rearrange("p (k f) -> p k f", k=KC)
                m = ENDS[n] - 2
                for t in range(TT):
                    free(m + t)
                    for k in range(KC):
                        mm = pe.matmul(psum[:, (m + t) % 3, :], lhs[:, k, t * P:(t + 1) * P], w[:, k, :],
                                       start=(k == 0), stop=(k == KC - 1))
                    mm.then_inc(tile_done, 1)

            def turn(i, src=hs):
                pe.wait_ge(hs_ready, 2 * (i + 1))
                for b in range(4):
                    for k in range(2):
                        for t in range(TT):
                            c = (2 * b + k) * P
                            mm = pe.transpose(psum[:, 4 + b, k * T + t * P:k * T + (t + 1) * P],
                                              src[:, t, c:c + P], ident)
                    mm.then_inc(turned, 1)

            pe.wait_ge(small_loaded, 32)
            turn(0)
            pe.wait_ge(xT_ready, 4)
            for s in range(4):
                features("a_in", s, xT)
            w = slot_in(FIRST["a_gates"])
            m = tile0("a_gates")
            for g in range(8):
                pe.wait_ge(conv_ready, min(2 * (g % 4) + 2, 8))
                bank_free(m + g)
                for f in range(2):
                    j = 2 * g + f
                    mm = pe.matmul(psum[:, (m + g) % 3, f * T:(f + 1) * T], w[:, j * P:(j + 1) * P],
                                   xc[:, j % 8, :], start=True, stop=True)
                mm.then_inc(tile_done, 1)
            pe.wait_ge(gated_ready, 1)
            for s in range(2):
                tokens("a_out", s, lru[5])

            def peer(l, i):
                turn(i)
                pe.wait_ge(xT_ready, 4 * (i + 1) + 4 * l)
                for s in range(4):
                    features(f"peer_q{l}", s, xT)
                w = slot_in(FIRST[f"peer_keys{l}"])
                m = tile0(f"peer_keys{l}")
                pe.wait_ge(act_took, TILE_NTH[m - 1])
                for g in range(8):
                    bank_free(m + g)
                    for f in range(4):
                        j = 4 * (g % 4) + f
                        mm = pe.matmul(psum[:, (m + g) % 3, f * P:(f + 1) * P], qT[:, j, (g // 4) * P:(g // 4 + 1) * P],
                                       w[:, j * NK:(j + 1) * NK], start=True, stop=True)
                    mm.then_inc(tile_done, 1)
                n0, m0 = FIRST[f"peer_u{l}"], tile0(f"peer_u{l}")
                with pe.Fori(0, 10) as it:
                    def free(m):
                        pe.wait_ge(act_took, it * 6 + TILE_NTH[m - 3])
                    for s in range(RING):
                        features(None, s, xT, free=free, extra=it * 16, n=n0 + s)
                for s in range(30, 32):
                    features(f"peer_u{l}", s, xT)
                pe.wait_ge(pick_ready, l + 1)
                for r in range(3):
                    for t in range(TT):
                        c = (r % 2) * T + t * P
                        mm = pe.transpose(psum[:, 4 + r // 2, c:c + P], pick[:, r, t, :], ident)
                mm.then_inc(pick_turned, 1)
                pe.wait_ge(pickT_ready, l + 1)
                with pe.Fori(0, 16) as it:
                    for g in range(4):
                        pe.wait_ge(hot_ready, it * 4 + (64 * l + g + 1))
                        for k in range(4):
                            mm = pe.matmul(psum[:, 4 + g, k * P:(k + 1) * P], hot[:, g % 2, 0, k, :],
                                           hot[:, g % 2, 1, k, :], start=True, stop=True)
                        mm.then_inc(wmat_done, 1)
                n0 = FIRST[f"peer_v{l}"]

                def v_slot(s, n, at, extra=0, first=False, last=False):
                    pe.wait_ge(vstage_ready, at)
                    w = slot_in(n, extra)
                    for e in range(4):
                        for t in range(TT):
                            for c in range(2):
                                mm = pe.matmul(psum[:, 4 + 2 * t + c, :],
                                               vstage[:, s % 2, e * T + t * P:e * T + (t + 1) * P],
                                               w[:, e * D + c * 512:e * D + (c + 1) * 512],
                                               start=first and e == 0, stop=last and e == 3, skip_group_check=True)
                        if e % 2:
                            mm.then_inc(tile_done, 1)

                for s in range(2):
                    v_slot(s, n0 + s, 32 * l + s + 1, first=(s == 0))
                with pe.Fori(0, 4) as it:
                    for s in range(2, 8):
                        v_slot(s, n0 + s, it * 6 + (32 * l + s + 1), extra=it * 32)
                for s in range(26, 32):
                    v_slot(s, n0 + s, 32 * l + s + 1, last=(s == 31))

            def ple(l, i):
                turn(i)
                pe.wait_ge(xT_ready, 4 * (i + 1) + 4 * l)
                for s in range(2):
                    tokens(f"ple_gate{l}", s, xT)
                pe.wait_ge(p_loaded, 16 * (l + 1))
                w = slot_in(FIRST[f"ple_proj{l}"])[:, 0:2 * D].rearrange("p (k f) -> p k f", k=2)
                m = tile0(f"ple_proj{l}")
                for g in range(4):
                    bank_free(m + g)
                    for k in range(2):
                        mm = pe.matmul(psum[:, (m + g) % 3, :], pT[:, k, (g // 2) * P:(g // 2 + 1) * P],
                                       w[:, k, (g % 2) * 512:(g % 2 + 1) * 512], start=(k == 0), stop=(k == 1))
                    mm.then_inc(tile_done, 1)

            peer(0, 1)
            ple(0, 2)

            turn(3)
            pe.wait_ge(xT_ready, 20)
            for s in range(2):
                features("kv", s, xT)
            for s in range(2, 4):
                tokens("kv", s, xT)
            for s in range(2):
                features("bq", s, xT2)
            pe.wait_ge(act_took, TILE_NTH[tile0("bo") - 1])
            pe.wait_ge(late_loaded, 16)
            for a in range(HEADS):
                if a >= 4:
                    pe.wait_ge(lm_ready, a - 3)
                r = slice(64 * (a % 2), 64 * (a % 2) + 64)
                z = psum[:, 4 + a % 4, 0:384]
                pe.matmul(z[:, 0:256], kT[r, a // 2, 0:128], qbT[r, a // 2, :], start=True, stop=True)
                pe.matmul(z[:, 256:384], kT[r, a // 2, 128:256], qbT[r, a // 2, 128:256], start=True, stop=True,
                          ).then_inc(z_done, 1)
            tri, ones = late[:, C_TRI:C_TRI + P], late[:, C_ONES:C_ONES + P]
            for a in range(HEADS):
                pe.wait_ge(lm_ready, min(a + 13, HEADS))
                if a >= 4:
                    pe.wait_ge(aexp_in, a - 3)
                z = psum[:, 4 + a % 4, 0:384]
                pe.matmul(z[:, 128:256], ones, lm[:, a, 256:384], start=True, stop=False, skip_group_check=True)
                pe.matmul(z, tri, lm[:, a, :], start=False, stop=True, skip_group_check=True).then_inc(suffix_done, 1)
            for c in range(HEADS // 2):
                pe.wait_ge(a_ready, 2 * c + 2)
                if c >= 4:
                    pe.wait_ge(o_taken, c - 3)
                else:
                    pe.wait_ge(aexp_in, HEADS)
                for s in range(2):
                    a = 2 * c + s
                    o = psum[64 * s:64 * s + 64, 4 + c % 4, 0:256]
                    pe.matmul(o[:, 128:256], v_sb[:, 1, a * 64:a * 64 + 64], w_sb[:, a, 256:384],
                              start=True, stop=False, skip_group_check=True)
                    mm = pe.matmul(o, v_sb[:, 0, a * 64:a * 64 + 64], w_sb[:, a, 0:256],
                                   start=False, stop=True, skip_group_check=True)
                mm.then_inc(o_done, 1)
            pe.wait_ge(o_taken, HEADS // 2)
            for s in range(2):
                tokens("bo", s, oT)

            peer(1, 4)
            ple(1, 5)

            def spread(i):
                pe.wait_ge(diag_ready, i + 1)
                for k in range(KC):
                    mm = pe.matmul(psum[:, 4 + k // 4, (k % 4) * P:(k % 4 + 1) * P], late[:, C_ONES:C_ONES + P],
                                   diag[:, k, :], start=True, stop=True)
                mm.then_inc(row_done, 1)

            pe.wait_ge(late_loaded, 32)
            spread(0)
            pe.wait_ge(cond_ready, 1)
            for s in range(12):
                n = FIRST["ada"] + s
                w = slot_in(n).rearrange("p (k f) -> p k f", k=KC)
                m = ENDS[n] - 2
                for t in range(2):
                    bank_free(m + t)
                    for f in range(2):
                        c = (2 * t + f) * P
                        for k in range(KC):
                            mm = pe.matmul(psum[:, (m + t) % 3, f:f + 1], w[:, k, c:c + P], tiny[:, 0, k:k + 1],
                                           start=(k == 0), stop=(k == KC - 1))
                    mm.then_inc(tile_done, 1)
            turn(6)
            pe.wait_ge(xT_ready, 32)
            for s in range(7):
                (features if s in (0, 1, 3, 4) else tokens)("mix_in", s, xT)

            pe.wait_ge(act_took, TILE_NTH[tile0("mix_in") + 5])

            def dil_scores(a):
                if a >= 2:
                    pe.wait_ge(da_in, a - 1)
                r = slice(64 * (a % 2), 64 * (a % 2) + 64)
                z = psum[:, 4 + a % 2, 0:384]
                pe.matmul(z[:, 0:128], qaT[r, a // 2, 0:128], kaT[r, a // 2, 0:128], start=True, stop=True)
                pe.matmul(z[:, 128:384], qaT[r, a // 2, 128:256], kaT[r, a // 2, :], start=True, stop=True,
                          ).then_inc(da_done, 1)

            dil_scores(0)
            for a in range(DIL_HEADS):
                if a + 1 < DIL_HEADS:
                    dil_scores(a + 1)
                pe.wait_ge(da_p, a + 1)
                for j in range(3):
                    mm = pe.transpose(psum[:, 6, j * P:(j + 1) * P], em[:, a % 2, j * P:(j + 1) * P], ident)
                mm.then_inc(da_turned, 1)
                pe.wait_ge(da_copied, a + 1)
                if a:
                    pe.wait_ge(da_taken, a)
                c = slice(a * 64, a * 64 + 64)
                pe.matmul(psum[:, 7, 0:64], pmT[:, a % 2, 0:128], va[:, 0, c], start=True, stop=True)
                pe.matmul(psum[:, 7, 64:128], pmT[:, a % 2, 128:256], va[:, 0, c], start=True, stop=False)
                pe.matmul(psum[:, 7, 64:128], pmT[:, a % 2, 256:384], va[:, 1, c], start=False, stop=True).then_inc(
                    da_o, 1)
            pe.wait_ge(da_taken, DIL_HEADS)

            for a in range(REC_HEADS):
                pe.wait_ge(kd_ready, 3 * a + 3)
                if a:
                    pe.wait_ge(kdt_taken, a)
                for t in range(TT):
                    mm = pe.transpose(psum[:, 4, t * P:(t + 1) * P], kd[:, a, t * P:(t + 1) * P], ident)
                mm.then_inc(kdt_done, 1)
                if a:
                    pe.wait_ge(am_taken, 2 * a)
                for t in range(TT):
                    mm = pe.matmul(psum[:, 5, t * P:(t + 1) * P], ke[:, a, t * P:(t + 1) * P],
                                   qe[:, a, t * P:(t + 1) * P], start=True, stop=True)
                mm.then_inc(am_done, 1)
            pe.wait_ge(kdt_taken, REC_HEADS)
            pe.wait_ge(am_taken, 2 * REC_HEADS)
            for c in range(7):
                if c:
                    pe.wait_ge(state_ready, 4 * c)
                for a in range(REC_HEADS):
                    r = slice(CHUNK * (c % 4), CHUNK * (c % 4) + CHUNK)
                    mm = pe.matmul(psum[:, 4 + c % 2, a * P:(a + 1) * P], kdt[r, a, c // 4, :],
                                   vr[r, c // 4, a * P:(a + 1) * P], start=True, stop=True)
                mm.then_inc(delta_done, 1)
                if c in (2, 6):
                    t = c // 4
                    pe.wait_ge(state_ready, 4 * (c + 1))
                    for a in range(REC_HEADS):
                        o = psum[:, 6 + t, a * P:(a + 1) * P]
                        pe.matmul(o, am[:, a, t, :], vr[:, t, a * P:(a + 1) * P], start=True, stop=False,
                                  skip_group_check=True)
                        for j in range(4):
                            n = 4 * t + j
                            if n:
                                mm = pe.matmul(psum[CHUNK * j:CHUNK * (j + 1), 6 + t, a * P:(a + 1) * P],
                                               qe[:, a, n * CHUNK:(n + 1) * CHUNK], states[:, n % 4, a, :],
                                               start=False, stop=(j == 3), skip_group_check=True)
                    mm.then_inc(ro_done, 1)
            turn(7, ylow)
            pe.wait_ge(xT_ready, 36)
            for s in range(2):
                tokens("mix_out", s, xT)
            spread(1)
            turn(8)
            spread(2)
            spread(3)
            pe.wait_ge(xT_ready, 40)

            pe.wait_ge(moe_loaded, 80)
            for t in range(TT):
                for k in range(KC):
                    pe.matmul(psum[:, 3, t * E2:(t + 1) * E2], xT[:, k, t * P:(t + 1) * P], wr[:, k, :],
                              start=(k == 0), stop=False)
                mm = pe.matmul(psum[:, 3, t * E2:(t + 1) * E2], late[0:1, C_ONES:C_ONES + P], br[0:1, :],
                               start=False, stop=True)
            mm.then_inc(logits_done, 1)
            pe.wait_ge(member_ready, 1)
            strict, ones = late[:, C_MASK:C_MASK + P], late[:, C_ONES:C_ONES + P]
            pe.matmul(psum[:, 3, 0:E2], strict, member[:, 0], start=True, stop=True)
            pe.matmul(psum[:, 3, E2:2 * E2], ones, member[:, 0], start=True, stop=False)
            pe.matmul(psum[:, 3, E2:2 * E2], strict, member[:, 1], start=False, stop=True)
            pe.matmul(psum[:, 3, 2 * E2:3 * E2], ones, member[:, 0], start=True, stop=False)
            pe.matmul(psum[:, 3, 2 * E2:3 * E2], ones, member[:, 1], start=False, stop=True).then_inc(ranks_done, 1)
            for t in range(TT):
                mm = pe.transpose(psum[0:E2, 4, t * P:(t + 1) * P], G[:, t, :], ident)
            mm.then_inc(gT_done, 1)

            def gather(bank):
                for k in range(KC):
                    for t in range(TT):
                        mm = pe.matmul(psum[:, bank(k // 4), (k % 4) * P:(k % 4 + 1) * P], hs[:, t, k * P:(k + 1) * P],
                                       S[:, t, :], start=(t == 0), stop=(t == TT - 1))
                    if k % 4 == 3:
                        yield mm

            pe.wait_ge(first_S, 1)
            for mm in gather(lambda b: 5 + b):
                mm.then_inc(gather0_done, 1)
            pe.wait_ge(gather0_taken, 2)
            for t in range(TT):
                for c in range(2):
                    pe.matmul(psum[:, 4 + 2 * t + c, :], gT[0:E2, t * P:(t + 1) * P],
                              bdn[0:E2, c * 512:(c + 1) * 512], start=True, stop=False, skip_group_check=True)

            def scatter(stop):
                for t in range(TT):
                    for c in range(2):
                        mm = pe.matmul(psum[:, 4 + 2 * t + c, :], SGT[:, t * P:(t + 1) * P], Y[:, c * 512:(c + 1) * 512],
                                       start=False, stop=stop, skip_group_check=True)
                return mm

            n0, m0 = FIRST["moe"], tile0("moe")
            n = pe.value_load(blocks[0:1, 0:1], min_val=E2, max_val=2 * E2)
            with pe.Fori(0, n) as i:
                def free(m):
                    j = m - m0
                    if j < 3:
                        pe.wait_ge(act_took, i * 5 + (TILE_NTH[m + 6] - 5))
                    elif TILE_ENGINE[m - 3] == "A":
                        pe.wait_ge(act_took, i * 5 + TILE_NTH[m - 3])
                    else:
                        pe.wait_ge(dve_took, i * 4 + TILE_NTH[m - 3])

                for s in range(4):
                    w = slot_in(n0 + s, i * 32).rearrange("p (k f) -> p k f", k=KC)
                    free(m0 + s)
                    for f in range(4):
                        for k in range(KC):
                            mm = pe.matmul(psum[:, (m0 + s) % 3, f * P:(f + 1) * P], w[:, k, f * P:(f + 1) * P],
                                           xgT[:, k, :], start=(k == 0), stop=(k == KC - 1))
                    mm.then_inc(tile_done, 1)
                    if s == 0:
                        pe.wait_ge(act_took, i * 5 + (TILE_NTH[m0 + 8] - 5))
                        scatter(False)
                pe.wait_ge(S_ready, i + 1)
                free(m0 + 4)
                for t in range(TT):
                    mm = pe.transpose(psum[:, (m0 + 4) % 3, t * P:(t + 1) * P], SG[:, t, :], ident)
                mm.then_inc(tile_done, 1)
                free(m0 + 5)
                free(m0 + 6)
                for mm in gather(lambda b: (m0 + 5 + b) % 3):
                    mm.then_inc(tile_done, 1)
                pe.wait_ge(act_ready, i * 4 + 4)
                for s in range(4, 6):
                    w = slot_in(n0 + s, i * 32).rearrange("p (k f) -> p k f", k=KC)
                    m = m0 + 3 + s
                    free(m)
                    for k in range(KC):
                        mm = pe.matmul(psum[:, m % 3, :], actT[:, k, :], w[:, k, :], start=(k == 0), stop=(k == KC - 1))
                    mm.then_inc(tile_done, 1)
            pe.wait_ge(act_took, n * 5 + (TILE_NTH[m0 + 8] - 5))
            scatter(True).then_inc(moe_done, 1)
            spread(4)

        @block.scalar
        def _(act):
            act.dma_start(small[:], d["small"]).then_inc(small_loaded, 16)
            act.dma_start(vecs[:], d["vecs"]).then_inc(small_loaded, 16)

            def tile_in(m, plus=0):
                act.wait_ge(tile_done, plus + (m + 1))
                return psum[:, m % 3, :]

            def root(i):
                act.wait_ge(var_ready, i + 1)
                act.activation(std[:], ms[:], ACT.Sqrt).then_inc(std_ready, 1)

            def two(x):
                return x.rearrange("p (a b) -> p a b", a=2)

            act.wait_ge(spl_ready, 1)
            act.activation(tiny[:, 1, :], tiny[:, 0, :], ACT.Exp, scale=-1.0).then_inc(expl_ready, 1)
            root(0)
            m = tile0("a_in")
            for g in range(4):
                act.activation(gy[:, 2 * g:2 * g + 2, :], two(tile_in(m + g)), ACT.Gelu_apprx_tanh).then_inc(act_took, 1)
            act.wait_ge(pads_ready, 1)
            for g in range(4, 8):
                act.activation(xb[:, 2 * g - 8:2 * g - 6, 3:3 + T], two(tile_in(m + g)), ACT.Copy).then_inc(act_took, 1)
            m = tile0("a_gates")
            for g in range(8):
                x = tile_in(m + g)
                for f in range(2):
                    j = 2 * g + f
                    i = act.activation(lru[j // 8][:, j % 8, :], x[:, f * T:(f + 1) * T], ACT.Sigmoid,
                                       bias=V8("b_r" if j < 8 else "b_i")[:, j % 8:j % 8 + 1])
                i.then_inc(act_took, 1)
            act.wait_ge(spl_ready, 2)
            act.drain()
            for a in range(KC):
                i = act.activation(lru[2][:, a, :], lru[0][:, a, :], ACT.Tanh, scale=tiny[:, 6, a:a + 1])
            i.then_inc(tanh_ready, 1)
            act.wait_ge(tanh_ready, 1)
            act.activation(lru[3], lru[2], ACT.Sqrt).then_inc(sqrt_ready, 1)

            def peer(l, i):
                root(i)
                m = tile0(f"peer_q{l}")
                for g in range(8):
                    act.activation(qT[:, 2 * g:2 * g + 2, :], two(tile_in(m + g)), ACT.Copy).then_inc(act_took, 1)
                m = tile0(f"peer_keys{l}")
                for g in range(8):
                    act.activation(scores[:, g // 4, 4 * (g % 4):4 * (g % 4) + 4, :],
                                   tile_in(m + g).rearrange("p (a b) -> p a b", a=4), ACT.Copy).then_inc(act_took, 1)
                m = tile0(f"peer_u{l}")
                flat = acts.rearrange("p a b -> p (a b)")
                with act.Fori(0, 9) as it:
                    for g in range(6):
                        act.activation(flat[:, bass.ds(it * (6 * 512) + g * 512, 512)], tile_in(m + g, it * 6),
                                       ACT.Gelu_apprx_tanh).then_inc(act_took, 1)
                for g in range(54, 64):
                    if g == 56:
                        act.wait_ge(topk_done, l + 1)
                    act.activation(flat[:, g * 512:(g + 1) * 512], tile_in(m + g),
                                   ACT.Gelu_apprx_tanh).then_inc(act_took, 1)
                act.wait_ge(gexp_in, l + 1)
                act.activation(cval[:], cval[:], ACT.Exp).then_inc(gexp_out, 1)
                act.wait_ge(gated_acts, 64 * (l + 1))
                mv = tile0(f"peer_v{l}")
                for s in range(2):
                    act.activation(vstage[:, s, :], flat[:, s * D:(s + 1) * D], ACT.Copy).then_inc(vstage_ready, 1)
                with act.Fori(0, 5) as it:
                    for s in range(2, 8):
                        act.wait_ge(tile_done, it * 12 + (mv + 2 * (s - 2) + 2))
                        act.activation(vstage[:, s % 2, :], flat[:, bass.ds(it * (6 * D) + s * D, D)],
                                       ACT.Copy).then_inc(vstage_ready, 1)

            def ple(l, i):
                act.wait_ge(vstage_ready, 32 * (l + 1))
                act.dma_start(pT, d["pT"][l]).then_inc(p_loaded, 16)
                act.dma_start(late, d["late"]).then_inc(late_loaded, 16)
                root(i)
                m = tile0(f"ple_gate{l}")
                for g in range(4):
                    act.activation(gate_sb[:, g % 2, (g // 2) * 512:(g // 2 + 1) * 512], tile_in(m + g),
                                   ACT.Sigmoid).then_inc(act_took, 1)

            peer(0, 1)
            ple(0, 2)

            root(3)
            m = tile0("kv")
            for g in range(4):
                act.activation(kT[:, 2 * g:2 * g + 2, :], two(tile_in(m + g)), ACT.Copy).then_inc(act_took, 1)
            for g in range(4, 8):
                act.activation(v_sb[:, g % 2, (g - 4) // 2 * 512:(g - 4) // 2 * 512 + 512], tile_in(m + g),
                               ACT.Copy).then_inc(act_took, 1)
            m = tile0("bq")
            for g in range(4):
                act.activation(qbT[:, 2 * g:2 * g + 2, :], two(tile_in(m + g)), ACT.Copy).then_inc(act_took, 1)
            for a in range(HEADS):
                act.wait_ge(z_done, a + 1)
                if a >= 2:
                    act.wait_ge(lm_ready, a - 1)
                z = psum[:, 4 + a % 4, 0:384]
                act.activation(za[:, 0, a % 2, :], z, ACT.Abs).then_inc(zabs_ready, 1)
                act.wait_ge(zabs_ready, 2 * a + 1)
                act.activation(za[:, 1, a % 2, :], za[:, 0, a % 2, :], ACT.Exp, scale=-SC).then_inc(zabs_ready, 1)
                act.wait_ge(zabs_ready, 2 * a + 2)
                act.activation(zl[:, a % 2, :], za[:, 1, a % 2, :], ACT.Ln, bias=1.0).then_inc(zlog_ready, 1)
            for a in range(HEADS):
                act.wait_ge(aexp_in, a + 1)
                act.activation(w_sb[:, a, :], w_sb[:, a, :], ACT.Exp).then_inc(aexp_out, 1)
            for c in range(HEADS // 2):
                act.wait_ge(o_done, c + 1)
                act.activation(oT[:, c, :], psum[:, 4 + c % 4, 0:256], ACT.Copy).then_inc(o_taken, 1)

            peer(1, 4)
            ple(1, 5)

            act.activation(tiny[:, 1, :], V8("c"), ACT.Sigmoid).then_inc(cond_sig, 1)
            root(6)
            root(7)
            m = tile0("mix_in")
            for g in range(2):
                act.activation(qaT[:, 2 * g:2 * g + 2, :], two(tile_in(m + g)), ACT.Copy).then_inc(act_took, 1)
            for g in range(2):
                act.activation(kaT[:, 2 * g:2 * g + 2, :], two(tile_in(m + 2 + g)), ACT.Copy).then_inc(act_took, 1)
            for g in range(2):
                act.activation(va[:, g, :], tile_in(m + 4 + g), ACT.Copy).then_inc(act_took, 1)
            for g in range(2):
                act.activation(qrT[:, 2 * g:2 * g + 2, :], two(tile_in(m + 6 + g)), ACT.Sigmoid).then_inc(silu_sig, 1)
            for g in range(2):
                act.activation(frT[:, 2 * g:2 * g + 2, :], two(tile_in(m + 8 + g)), ACT.Sigmoid).then_inc(act_took, 1)
            for g in range(2):
                act.activation(vr[:, g, :], tile_in(m + 10 + g), ACT.Copy).then_inc(act_took, 1)
            for g in range(2):
                act.activation(gr[:, g, :], tile_in(m + 12 + g), ACT.Sigmoid).then_inc(silu_sig, 1)
            for a in range(DIL_HEADS):
                act.wait_ge(da_in, a + 1)
                x, y = sm[:, a % 2, :], em[:, a % 2, :]
                act.activation(y[:, 0:128], x[:, 0:128], ACT.Exp, bias=dnum[:, a, 0:1])
                act.activation(y[:, 128:384], x[:, 128:384], ACT.Exp, bias=dnum[:, a, 1:2]).then_inc(da_exp, 1)
                act.wait_ge(da_turned, a + 1)
                act.activation(pmT[:, a % 2, :], psum[:, 6, 0:384], ACT.Copy).then_inc(da_copied, 1)
            act.wait_ge(lb_in, 1)
            act.activation(tiny[:, 3, 0:4], tiny[:, 2, 0:4], ACT.Sigmoid).then_inc(lb_sig, 1)
            act.wait_ge(f_ready, 1)
            act.activation(b_, f_, ACT.Ln).then_inc(logf_ready, 1)
            act.wait_ge(b_ready, 1)
            act.activation(eb, b_, ACT.Exp)
            act.activation(ke, b_, ACT.Exp, scale=-1.0)
            act.activation(decay, blast, ACT.Exp)
            act.activation(kd, kd, ACT.Exp).then_inc(eb_ready, 1)
            for a in range(REC_HEADS):
                act.wait_ge(kdt_done, a + 1)
                act.activation(kdt[:, a], two(psum[:, 4, 0:T]), ACT.Copy).then_inc(kdt_taken, 1)
            act.wait_ge(lb_in, 2)
            act.activation(hst, hst, ACT.Sqrt).then_inc(lb_sig, 1)
            root(8)
            root(9)
            act.wait_ge(gexp2_in, 1)
            act.activation(tk[:, 16:32], tk[:, 16:32], ACT.Exp).then_inc(gexp2_out, 1)
            for b in range(2):
                act.wait_ge(gather0_done, b + 1)
                act.activation(xgT[:, 4 * b:4 * b + 4, :], psum[:, 5 + b, :].rearrange("p (a b) -> p a b", a=4),
                               ACT.Copy).then_inc(gather0_taken, 1)
            m = tile0("moe")
            act.wait_ge(blocks_ready, 1)
            n = act.value_load(blocks[0:1, 0:1], min_val=E2, max_val=2 * E2)
            with act.Fori(0, n) as i:
                for s in range(4):
                    act.wait_ge(dve_took, i * 4 + TILE_NTH[m + s])
                    act.activation(sgm[:, s % 2], xg[:, s % 2], ACT.Sigmoid, scale=1.702).then_inc(sig_ready, 1)
                act.activation(SGT, tile_in(m + 4, i * BLOCK_TILES)[:, 0:T], ACT.Copy).then_inc(act_took, 1)
                for b in range(2):
                    act.activation(xgT[:, 4 * b:4 * b + 4, :],
                                   tile_in(m + 5 + b, i * BLOCK_TILES).rearrange("p (a b) -> p a b", a=4),
                                   ACT.Copy).then_inc(act_took, 1)
                for c in range(2):
                    act.activation(Y[:, c * 512:(c + 1) * 512], tile_in(m + 7 + c, i * BLOCK_TILES),
                                   ACT.Copy).then_inc(act_took, 1)
            root(10)

        @block.vector
        def _(dve):
            def tile_in(m, plus=0):
                dve.wait_ge(tile_done, plus + (m + 1))
                return psum[:, m % 3, :]

            def two(x):
                return x.rearrange("p (a b) -> p a b", a=2)

            def wide(v, n):
                return v.unsqueeze(2).to_broadcast([P, v.shape[1], n])

            def scales(i, src):
                for t in range(TT):
                    dve.tensor_tensor_reduce(out=hs[:, t, :], in0=src[:, t, :], in1=src[:, t, :], scale=1.0, scalar=0.0,
                                             op0=ALU.mult, op1=ALU.add, accum_out=ss[:, t:t + 1])
                dve.drain()
                dve.tensor_scalar(ms[:], ss[:], 1.0 / D, EPS, ALU.mult, ALU.add).then_inc(var_ready, 1)
                dve.wait_ge(std_ready, i + 1)
                dve.reciprocal(rstd[:], std[:])
                dve.drain()

            def scaled():
                for t in range(TT):
                    dve.tensor_scalar(hs[:, t, :], h[:, t, :], rstd[:, t:t + 1], None, ALU.mult).then_inc(hs_ready, 1)

            def gains(i, gain, gain2=None, shift=None):
                for b in range(4):
                    dve.wait_ge(turned, 4 * i + b + 1)
                    x = two(psum[:, 4 + b, :])
                    o = xT[:, 2 * b:2 * b + 2, :]
                    if gain2 is not None:
                        dve.tensor_tensor(xT2[:, 2 * b:2 * b + 2, :], x, wide(gain2[:, 2 * b:2 * b + 2], T), ALU.mult)
                    j = dve.tensor_tensor(o, x, wide(gain[:, 2 * b:2 * b + 2], T), ALU.mult)
                    if shift is None:
                        j.then_inc(xT_ready, 1)
                if gain2 is not None:
                    dve.drain().then_inc(xT_ready, 4)
                if shift is not None:
                    dve.drain()
                    for b in range(4):
                        o = xT[:, 2 * b:2 * b + 2, :]
                        dve.tensor_tensor(o, o, wide(shift[:, 2 * b:2 * b + 2], T), ALU.add).then_inc(xT_ready, 1)

            dve.wait_ge(small_loaded, 32)
            nl, t0, e1, s1, s2, pl = (tiny[:, i, :] for i in (2, 0, 1, 3, 4, 5))
            dve.tensor_scalar(nl, V8("lam"), -1.0, None, ALU.mult)
            dve.drain()
            dve.tensor_tensor(t0, nl, V8("lam"), ALU.max).then_inc(spl_ready, 1)
            dve.memset(xb[:, :, 0:3], 0.0).then_inc(pads_ready, 1)
            dve.wait_ge(expl_ready, 1)
            dve.tensor_scalar(s1, e1, 2.0, None, ALU.add)
            dve.drain()
            dve.reciprocal(s2, s1)
            dve.drain()
            dve.tensor_tensor(s1, e1, s2, ALU.mult)
            dve.drain()
            dve.tensor_tensor(s2, s1, s1, ALU.mult)
            dve.memset(pl, 1.0 / 17.0)
            dve.drain()
            for k in (15, 13, 11, 9, 7, 5, 3, 1):
                dve.tensor_tensor(pl, pl, s2, ALU.mult)
                dve.drain()
                dve.tensor_scalar(pl, pl, 1.0 / k, None, ALU.add)
                dve.drain()
            dve.tensor_tensor(pl, pl, s1, ALU.mult)
            dve.tensor_scalar(nl, nl, 0.0, 4.0, ALU.max, ALU.mult)
            dve.drain()
            dve.scalar_tensor_tensor(tiny[:, 6, :], pl, 8.0, nl, ALU.mult, ALU.add).then_inc(spl_ready, 1)

            dve.wait_ge(x_loaded, 16)
            scales(0, h)
            scaled()
            gains(0, V8("norm_mix0"))
            for g in range(4):
                dve.wait_ge(act_took, 5 + g)
                for j in range(4):
                    for a in (2 * g, 2 * g + 1):
                        x, o = xb[:, a, 3 - j:3 - j + T], xc[:, a, :]
                        w = V8(f"conv{3 - j}")[:, a:a + 1]
                        if j == 0:
                            dve.tensor_scalar(o, x, w, V8("conv_b")[:, a:a + 1], ALU.mult, ALU.add)
                        else:
                            i = dve.scalar_tensor_tensor(o, x, w, o, ALU.mult, ALU.add)
                            if j == 3:
                                i.then_inc(conv_ready, 1)
                    if j < 3:
                        dve.drain()
            dve.wait_ge(act_took, TILE_NTH[tile0("a_gates") + 7])
            dve.wait_ge(conv_ready, 8)
            dve.tensor_tensor(lru[4], lru[1], xc, ALU.mult)
            dve.wait_ge(tanh_ready, 1)
            dve.tensor_scalar(lru[0], lru[2], 1.0, None, ALU.add)
            dve.drain()
            dve.reciprocal(lru[1], lru[0])
            dve.tensor_scalar(lru[5], lru[2], -1.0, 1.0, ALU.mult, ALU.add)
            dve.drain()
            dve.tensor_tensor(lru[0], lru[5], lru[1], ALU.mult)
            dve.tensor_tensor(lru[4], lru[4], lru[1], ALU.mult)
            dve.wait_ge(sqrt_ready, 1)
            dve.drain()
            dve.scalar_tensor_tensor(lru[1], lru[3], 2.0, lru[4], ALU.mult, ALU.mult)
            dve.drain()
            for a in range(KC):
                dve.tensor_tensor_scan(lru[4][:, a, :], lru[0][:, a, :], lru[1][:, a, :], 0.0, ALU.mult, ALU.add)
            dve.drain()
            dve.tensor_tensor(lru[5], lru[4], gy, ALU.mult).then_inc(gated_ready, 1)

            def add_to_residual(stage):
                m = tile0(stage)
                for g in range(4):
                    x = tile_in(m + g)
                    o = h[:, g % 2, (g // 2) * 512:(g // 2 + 1) * 512]
                    dve.tensor_tensor(o, o, x, ALU.add).then_inc(dve_took, 1)
                dve.drain()

            add_to_residual("a_out")

            def peer(l, i):
                scales(i, h)
                scaled()
                gains(i, V8(f"norm_ffn{l}"))
                dve.wait_ge(act_took, TILE_NTH[tile0(f"peer_keys{l}") + 7])
                sflat = scores.rearrange("p a b c -> p (a b c)")
                cvflat = cval[:].rearrange("p a b c -> p (a b c)")
                pflat = [pick[:, r].rearrange("p a b -> p (a b)") for r in range(3)]
                iota16 = iota[:, 0:TOPK]
                wflat, cflat = work[:].rearrange("p a b -> p (a b)"), cand[:].rearrange("p a b -> p (a b)")

                def best16(vals, idx, src, scratch):
                    dve.max(vals[:, 0:8], src)
                    dve.drain()
                    dve.max_index(idx[:, 0:8], vals[:, 0:8], src)
                    dve.match_replace(out=scratch, in_to_replace=vals[:, 0:8], in_values=src, imm_value=NEG)
                    dve.drain()
                    dve.max(vals[:, 8:16], scratch)
                    dve.drain()
                    dve.max_index(idx[:, 8:16], vals[:, 8:16], scratch)

                with dve.Fori(0, TT * PH) as it:
                    dve.tensor_copy(keys_in[:].rearrange("p a b -> p (a b)"), sflat[:, bass.ds(it * 256, 256)])
                    dve.drain()
                    for half in range(2):
                        best16(sv[:, half, :], si[:, half, :], keys_in[:, half, :], wflat[:, half * P:(half + 1) * P])
                    dve.drain()
                    dve.tensor_copy(sif[:], si[:])
                    dve.tensor_tensor(cand[:], sv[:, 0, :].unsqueeze(2).to_broadcast([P, TOPK, TOPK]),
                                      sv[:, 1, :].unsqueeze(1).to_broadcast([P, TOPK, TOPK]), ALU.add)
                    dve.drain()
                    best16(cv, ci, cflat, wflat)
                    dve.drain()
                    dve.tensor_copy(cvflat[:, bass.ds(it * TOPK, TOPK)], cv[:])
                    dve.tensor_single_scalar(cab[:, 0, :], ci[:], 4, ALU.logical_shift_right)
                    dve.tensor_single_scalar(cab[:, 1, :], ci[:], 15, ALU.bitwise_and)
                    dve.drain()
                    dve.tensor_copy(cabf[:], cab[:])
                    dve.drain()
                    for half in range(2):
                        w = work if half else cand
                        dve.tensor_tensor(w[:], iota16.unsqueeze(1).to_broadcast([P, TOPK, TOPK]),
                                          cabf[:, half, :].unsqueeze(2).to_broadcast([P, TOPK, TOPK]), ALU.is_equal)
                    dve.drain()
                    for half in range(2):
                        w = work if half else cand
                        dve.tensor_tensor(w[:], w[:], sif[:, half, :].unsqueeze(1).to_broadcast([P, TOPK, TOPK]),
                                          ALU.mult)
                    dve.drain()
                    for half in range(2):
                        w = work if half else cand
                        dve.tensor_reduce(pflat[half][:, bass.ds(it * TOPK, TOPK)], w[:], AX.X, ALU.add)
                    dve.drain()
                for t in range(TT):
                    dve.tensor_tensor(pick[:, 2, t].rearrange("p (a b) -> p a b", a=PH), cval[:, t],
                                      cval[:, t, :, 0:1].to_broadcast([P, PH, TOPK]), ALU.subtract)
                dve.drain().then_inc(topk_done, 1)
                dve.tensor_copy(cval[:].rearrange("p a b c -> p (a b c)"), pflat[2]).then_inc(gexp_in, 1)
                dve.wait_ge(gexp_out, l + 1)
                sums = tiny[:, 7:9, :]
                for t in range(TT):
                    dve.tensor_reduce(sums[:, t, :], cval[:, t], AX.X, ALU.add)
                dve.drain()
                dve.reciprocal(sums, sums)
                dve.drain()
                for t in range(TT):
                    dve.tensor_tensor(pick[:, 2, t].rearrange("p (a b) -> p a b", a=PH), cval[:, t],
                                      sums[:, t, :].unsqueeze(2).to_broadcast([P, PH, TOPK]), ALU.mult)
                dve.drain().then_inc(pick_ready, 1)
                dve.wait_ge(pick_turned, l + 1)
                dve.tensor_copy(pickT[:, 0:2, :], two(psum[:, 4, :]))
                dve.tensor_copy(pickT[:, 2, :], psum[:, 5, 0:T])
                dve.drain().then_inc(pickT_ready, 1)
                dve.wait_ge(act_took, TILE_NTH[tile0(f"peer_v{l}") - 1])
                dve.wait_ge(tile_done, tile0(f"peer_v{l}"))
                kflat = pickT[:].rearrange("p a b -> p (a b)")

                def one_hot(g, at):
                    for k in range(4):
                        dve.tensor_scalar(hot[:, g % 2, 0, k, :], iota, kflat[:, bass.ds(at + k, 1)], None, ALU.is_equal)
                        i = dve.tensor_scalar(hot[:, g % 2, 1, k, :], iota, kflat[:, bass.ds(at + (T + k), 1)],
                                              kflat[:, bass.ds(at + (2 * T + k), 1)], ALU.is_equal, ALU.mult)
                    i.then_inc(hot_ready, 1)

                def gate(g, at, n):
                    dve.wait_ge(wmat_done, n)
                    x = acts[:, :, bass.ds(at, 4)]
                    dve.tensor_tensor(x, x, psum[:, 4 + g % 4, :].rearrange("p (t i) -> p i t", t=4),
                                      ALU.mult).then_inc(gated_acts, 1)

                one_hot(0, 0)
                with dve.Fori(0, 15) as it:
                    for g in range(4):
                        one_hot(g + 1, it * 16 + 4 * (g + 1))
                        gate(g, it * 16 + 4 * g, it * 4 + (64 * l + g + 1))
                for g in range(60, 64):
                    if g < 63:
                        one_hot(g + 1, 4 * (g + 1))
                    gate(g, 4 * g, 64 * l + g + 1)
                dve.wait_ge(tile_done, ENDS[FIRST[f"peer_v{l}"] + 31])
                for t in range(TT):
                    for c in range(2):
                        o = h[:, t, c * 512:(c + 1) * 512]
                        dve.tensor_tensor(o, o, psum[:, 4 + 2 * t + c, :], ALU.add)
                dve.drain()

            def ple(l, i):
                scales(i, h)
                scaled()
                gains(i, V8(f"norm_ple{l}"))
                m = tile0(f"ple_proj{l}")
                dve.wait_ge(act_took, TILE_NTH[m - 1])
                for g in range(4):
                    c = slice((g % 2) * 512, (g % 2 + 1) * 512)
                    dve.tensor_tensor(ple_t[:, g // 2, c], tile_in(m + g), gate_sb[:, g // 2, c],
                                      ALU.mult).then_inc(dve_took, 1)
                dve.drain()
                dve.tensor_tensor(h[:], h[:], ple_t, ALU.add)
                dve.drain()

            peer(0, 1)
            ple(0, 2)

            scales(3, h)
            scaled()
            gains(3, V8("kv_norm"), gain2=V8("norm_mix1"))
            dve.wait_ge(late_loaded, 16)
            mask = late[:, C_MASK:C_MASK + 384]
            for a in range(HEADS):
                z = psum[:, 4 + a % 4, 0:384]
                dve.wait_ge(zlog_ready, a + 1)
                pos = za[:, 2, a % 2, :]
                dve.tensor_scalar(pos, z, SC, 0.0, ALU.mult, ALU.max)
                dve.drain()
                dve.tensor_tensor(pos, pos, zl[:, a % 2, :], ALU.add)
                dve.drain()
                dve.scalar_tensor_tensor(w_sb[:, a, :], z, SC, pos, ALU.mult, ALU.subtract)
                dve.tensor_tensor(lm[:, a, :], pos, mask, ALU.mult)
                dve.drain().then_inc(lm_ready, 1)

            def masked(a):
                dve.wait_ge(aexp_out, a + 1)
                dve.tensor_tensor(w_sb[:, a, :], w_sb[:, a, :], mask, ALU.mult).then_inc(a_ready, 1)

            for a in range(HEADS):
                dve.wait_ge(suffix_done, a + 1)
                dve.tensor_tensor(w_sb[:, a, :], w_sb[:, a, :], psum[:, 4 + a % 4, 0:384],
                                  ALU.subtract).then_inc(aexp_in, 1)
                if a:
                    masked(a - 1)
            masked(HEADS - 1)
            add_to_residual("bo")

            peer(1, 4)
            ple(1, 5)

            def spread(i, vec, row=row):
                for k in range(KC):
                    j = dve.tensor_scalar(diag[:, k, :], ident, vec[:, k:k + 1], None, ALU.mult)
                j.then_inc(diag_ready, 1)
                dve.wait_ge(row_done, i + 1)
                dve.tensor_copy(row.rearrange("p (a b) -> p a b", a=2), psum[:, 4:6, :])
                dve.drain()

            dve.wait_ge(late_loaded, 32)
            spread(0, V8("final_norm"))
            scales(6, h)
            for t in range(TT):
                dve.scalar_tensor_tensor(h[:, t, :], h[:, t, :], rstd[:, t:t + 1], row, ALU.mult, ALU.mult)
            dve.wait_ge(cond_sig, 1)
            dve.tensor_tensor(tiny[:, 0, :], tiny[:, 1, :], V8("c"), ALU.mult).then_inc(cond_ready, 1)
            m = tile0("ada")
            avec = vecs[:, V["ada0"]:V["ada0"] + 6, :].rearrange("p a b -> p (a b)")
            for g in range(24):
                x = tile_in(m + g)
                dve.tensor_tensor(modv[:, 2 * g:2 * g + 2], x[:, 0:2], avec[:, 2 * g:2 * g + 2],
                                  ALU.add).then_inc(dve_took, 1)
            dve.drain()
            shift_m, scale_m, gate_m, shift_f, scale_f, gate_f = (modv[:, 8 * i:8 * i + 8] for i in range(6))
            gm, gf, rm, rf = (tiny[:, i, :] for i in (9, 10, 11, 12))
            dve.scalar_tensor_tensor(gm, scale_m, 1.0, V8("g_pre_mix"), ALU.add, ALU.mult)
            dve.scalar_tensor_tensor(gf, scale_f, 1.0, V8("g_pre_ffn"), ALU.add, ALU.mult)
            dve.tensor_tensor(rm, gate_m, V8("g_post_mix"), ALU.mult)
            dve.tensor_tensor(rf, gate_f, V8("g_post_ffn"), ALU.mult)
            dve.drain()
            scales(7, h)
            scaled()
            gains(6, gm, shift=shift_m)
            m = tile0("mix_in")
            for g in range(2):
                dve.wait_ge(silu_sig, g + 1)
                o = qrT[:, 2 * g:2 * g + 2, :]
                dve.tensor_tensor(o, o, two(psum[:, (m + 6 + g) % 3, :]), ALU.mult).then_inc(dve_took, 1)
            for g in range(2):
                dve.wait_ge(silu_sig, g + 3)
                o = gr[:, g, :]
                dve.tensor_tensor(o, o, psum[:, (m + 12 + g) % 3, :], ALU.mult).then_inc(dve_took, 1)

            neg, cnt = late[:, C_NEG:C_NEG + 384], late[:, C_CNT:C_CNT + 384]
            for a in range(DIL_HEADS):
                dve.wait_ge(da_done, a + 1)
                x = sm[:, a % 2, :]
                y = em[:, a % 2, :]
                dve.scalar_tensor_tensor(x, psum[:, 4 + a % 2, 0:384], SC, neg, ALU.mult, ALU.add)
                dve.drain()
                dve.tensor_reduce(dnum[:, a, 0:1], x[:, 0:128], AX.X, ALU.max, negate=True)
                dve.tensor_reduce(dnum[:, a, 1:2], x[:, 128:384], AX.X, ALU.max, negate=True)
                dve.drain().then_inc(da_in, 1)
                dve.wait_ge(da_exp, a + 1)
                for t, c in ((0, slice(0, 128)), (1, slice(128, 384))):
                    dve.tensor_tensor_reduce(out=y[:, c], in0=y[:, c], in1=cnt[:, c], scale=1.0, scalar=0.0,
                                             op0=ALU.mult, op1=ALU.add, accum_out=dnum[:, a, 2 + t:3 + t])
                dve.drain().then_inc(da_p, 1)
                dve.reciprocal(dnum[:, a, 2:4], dnum[:, a, 2:4])
                dve.drain()
                dve.wait_ge(da_o, a + 1)
                dve.tensor_tensor(ylow[:, :, a * 64:a * 64 + 64], two(psum[:, 7, 0:128]), wide(dnum[:, a, 2:4], 64),
                                  ALU.mult).then_inc(da_taken, 1)

            dve.tensor_tensor(tiny[:, 2, 0:4], V8("lb")[:, 0:4], V8("lb")[:, 4:8], ALU.subtract).then_inc(lb_in, 1)
            dve.wait_ge(lb_sig, 1)
            dve.tensor_scalar(tiny[:, 4, 0:4], tiny[:, 3, 0:4], -1.0, 1.0, ALU.mult, ALU.add)
            dve.drain()
            dve.wait_ge(act_took, TILE_NTH[tile0("mix_in") + 11])
            for a in range(REC_HEADS):
                i = dve.tensor_scalar(f_[:, a, :], frT[:, a, :], tiny[:, 4, a:a + 1], tiny[:, 3, a:a + 1],
                                      ALU.mult, ALU.add)
            i.then_inc(f_ready, 1)
            dve.wait_ge(logf_ready, 1)
            reset = late[:, C_RESET:C_RESET + T]
            for a in range(REC_HEADS):
                dve.tensor_tensor_scan(frT[:, a, :], reset, b_[:, a, :], 0.0, ALU.mult, ALU.add)
            dve.drain()
            by_chunk = [v.rearrange("p a (n c) -> p a n c", c=CHUNK) for v in (frT, kd)]
            dve.tensor_copy(b_, frT)
            for a in range(REC_HEADS):
                dve.tensor_copy(blast[:, a, :].unsqueeze(2), by_chunk[0][:, a, :, CHUNK - 1:CHUNK])
            dve.drain()
            for a in range(REC_HEADS):
                dve.tensor_tensor(by_chunk[1][:, a], blast[:, a, :].unsqueeze(2).to_broadcast([P, 8, CHUNK]),
                                  by_chunk[0][:, a], ALU.subtract)
            dve.drain().then_inc(b_ready, 1)
            dve.tensor_scalar(f_, f_, -1.0, 1.0, ALU.mult, ALU.add)
            dve.drain()
            dve.wait_ge(eb_ready, 1)
            for a in range(REC_HEADS):
                dve.tensor_tensor(qe[:, a, :], qrT[:, a, :], eb[:, a, :], ALU.mult).then_inc(kd_ready, 1)
                dve.tensor_tensor(ke[:, a, :], ke[:, a, :], f_[:, a, :], ALU.mult).then_inc(kd_ready, 1)
                dve.tensor_tensor(kd[:, a, :], kd[:, a, :], f_[:, a, :], ALU.mult).then_inc(kd_ready, 1)
            dve.memset(am, 0.0)
            dve.drain()
            rmask = late[:, C_REC:C_REC + P].bitcast(I32)
            for a in range(REC_HEADS):
                dve.wait_ge(am_done, a + 1)
                for t in range(TT):
                    dve.copy_predicated(am[:, a, t, :], rmask, psum[:, 5, t * P:(t + 1) * P]).then_inc(am_taken, 1)
            for c in range(7):
                dve.wait_ge(delta_done, c + 1)
                for a in range(REC_HEADS):
                    x = psum[:, 4 + c % 2, a * P:(a + 1) * P]
                    o = states[:, (c + 1) % 4, a, :]
                    if c == 0:
                        dve.tensor_copy(o, x).then_inc(state_ready, 1)
                    else:
                        if c == 4:
                            dve.wait_ge(ro_done, 1)
                        dve.wait_ge(state_ready, 4 * (c - 1) + a + 1)
                        dve.scalar_tensor_tensor(o, states[:, c % 4, a, :], decay[:, a, c:c + 1], x, ALU.mult,
                                                 ALU.add).then_inc(state_ready, 1)
            dve.wait_ge(ro_done, 2)
            for t in range(TT):
                dve.tensor_copy(ylow[:, t, 512:1024], psum[:, 6 + t, :])
            dve.drain()
            dve.tensor_tensor(sq, ylow, ylow, ALU.mult)
            dve.drain()
            for t in range(TT):
                dve.tensor_reduce(hst[:, t * 12:t * 12 + 8], sq[:, t, 0:512].rearrange("p (a b) -> p a b", a=8),
                                  AX.X, ALU.add)
                dve.tensor_reduce(hst[:, t * 12 + 8:t * 12 + 12], sq[:, t, 512:1024].rearrange("p (a b) -> p a b", a=4),
                                  AX.X, ALU.add)
            dve.drain()
            for t in range(TT):
                for a, b, n in ((0, 8, 64), (8, 12, 128)):
                    o = hst[:, t * 12 + a:t * 12 + b]
                    dve.tensor_scalar(o, o, 1.0 / n, EPS, ALU.mult, ALU.add)
            dve.drain().then_inc(lb_in, 1)
            dve.wait_ge(lb_sig, 2)
            dve.reciprocal(hst, hst)
            dve.drain()
            for t in range(TT):
                for a, b, c0, n in ((0, 8, 0, 64), (8, 12, 512, 128)):
                    o = ylow[:, t, c0:c0 + 512].rearrange("p (a b) -> p a b", b=n)
                    dve.tensor_tensor(o, o, wide(hst[:, t * 12 + a:t * 12 + b], n), ALU.mult)
            dve.drain()
            for t in range(TT):
                o = ylow[:, t, 512:1024]
                dve.tensor_tensor(o, o, gr[:, t, :], ALU.mult)
            dve.drain().then_inc(hs_ready, 2)
            gains(7, V8("mix_norm"))
            m = tile0("mix_out")
            for g in range(4):
                dve.tensor_copy(ysb[:, g % 2, (g // 2) * 512:(g // 2 + 1) * 512], tile_in(m + g)).then_inc(dve_took, 1)
            dve.drain()
            spread(1, rm)
            scales(8, ysb)

            def add_row_scaled(src, out):
                for t in range(TT):
                    dve.scalar_tensor_tensor(src[:, t, :], src[:, t, :], rstd[:, t:t + 1], row, ALU.mult, ALU.mult)
                dve.drain()
                for t in range(TT):
                    i = dve.tensor_tensor(out[:, t, :], h[:, t, :], src[:, t, :], ALU.add)
                    if out is hs:
                        i.then_inc(y_ready, 1)
                dve.drain()

            add_row_scaled(ysb, h)
            scales(9, h)
            scaled()
            gains(8, gf, shift=shift_f)
            spread(2, gf)
            spread(3, shift_f, row2)
            for t in range(TT):
                dve.tensor_tensor(hs[:, t, :], hs[:, t, :], row, ALU.mult)
            dve.drain()
            for t in range(TT):
                dve.tensor_tensor(hs[:, t, :], hs[:, t, :], row2, ALU.add)
            dve.drain()

            dve.wait_ge(logits_done, 1)
            dve.tensor_copy(logit, psum[:, 3, 0:2 * E2].rearrange("p (a b) -> p a b", a=2))
            dve.drain()
            for t in range(TT):
                dve.max(tk[:, 8 * t:8 * t + 8], logit[:, t, :])
            dve.drain()
            for t in range(TT):
                dve.max_index(tki[:, 8 * t:8 * t + 8], tk[:, 8 * t:8 * t + 8], logit[:, t, :])
                dve.tensor_scalar(tk[:, 16 + 8 * t:24 + 8 * t], tk[:, 8 * t:8 * t + 8], tk[:, 8 * t:8 * t + 1], None,
                                  ALU.subtract)
            dve.drain().then_inc(gexp2_in, 1)
            dve.tensor_copy(tk[:, 32:48], tki)
            dve.wait_ge(gexp2_out, 1)
            for t in range(TT):
                dve.tensor_reduce(tk[:, 48 + t:49 + t], tk[:, 16 + 8 * t:20 + 8 * t], AX.X, ALU.add)
            dve.drain()
            dve.reciprocal(tk[:, 50:52], tk[:, 48:50])
            dve.drain()
            for t in range(TT):
                dve.tensor_scalar(tk[:, 16 + 8 * t:20 + 8 * t], tk[:, 16 + 8 * t:20 + 8 * t], tk[:, 50 + t:51 + t], None,
                                  ALU.mult)
            dve.memset(G, 0.0)
            dve.memset(member, 0.0)
            dve.memset(Y, 0.0)
            dve.memset(SGT, 0.0)
            dve.drain()
            i32 = late[:, C_IOTA32:C_IOTA32 + E2]
            for k in range(4):
                for t in range(TT):
                    dve.tensor_scalar(logit[:, t, :], i32, tk[:, 32 + 8 * t + k:33 + 8 * t + k], None, ALU.is_equal)
                dve.drain()
                for t in range(TT):
                    dve.tensor_tensor(member[:, t, :], member[:, t, :], logit[:, t, :], ALU.add)
                    dve.scalar_tensor_tensor(G[:, t, :], logit[:, t, :], tk[:, 16 + 8 * t + k:17 + 8 * t + k],
                                             G[:, t, :], ALU.mult, ALU.add)
                dve.drain()
            dve.drain().then_inc(member_ready, 1)
            dve.wait_ge(ranks_done, 1)
            ranks = psum[:, 3, 0:2 * E2].rearrange("p (a b) -> p a b", a=2)
            dve.memset(rank[:, :, 2 * E2:66], -1.0)
            dve.memset(G2[:, :, 2 * E2:66], 0.0)
            for t in range(TT):
                dve.scalar_tensor_tensor(rank[:, t, 0:E2], ranks[:, t, :], 1.0, member[:, t, :], ALU.add, ALU.mult)
                dve.tensor_copy(G2[:, t, 0:E2], G[:, t, :])
                dve.tensor_copy(G2[:, t, E2:2 * E2], G[:, t, :])
            dve.tensor_reduce(most[:, 0:1], psum[:, 3, 2 * E2:3 * E2], AX.X, ALU.max)
            dve.drain()
            for t in range(TT):
                dve.tensor_scalar(rank[:, t, 0:E2], rank[:, t, 0:E2], -1.0, None, ALU.add)
            dve.tensor_scalar(most[:, 1:2], most[:, 0:1], P + 0.5, float(E2), ALU.is_gt, ALU.mult)
            dve.drain()
            for t in range(TT):
                dve.tensor_scalar(rank[:, t, E2:2 * E2], rank[:, t, 0:E2], -float(P), None, ALU.add)
            dve.tensor_scalar(most[:, 2:3], most[:, 1:2], float(E2), None, ALU.add)
            dve.drain()
            dve.tensor_copy(blocks, most[:, 2:3])
            for t in range(TT):
                dve.tensor_scalar(S[:, t, :], iota, rank[:, t, 0:1], None, ALU.is_equal)
            dve.wait_ge(gT_done, 1)
            dve.tensor_copy(gT[0:E2, :], psum[0:E2, 4, 0:T])
            dve.drain().then_inc(first_S, 1)
            dve.drain().then_inc(blocks_ready, 1)

            m = tile0("moe")
            rflat, gflat = (v.rearrange("p a b -> p (a b)") for v in (rank, G2))
            bflat = bgu.rearrange("p a b -> p (a b)")
            n = dve.value_load(blocks[0:1, 0:1], min_val=E2, max_val=2 * E2)
            with dve.Fori(0, n) as i:
                for s in range(4):
                    x = tile_in(m + s, i * BLOCK_TILES)
                    for f in range(2):
                        dve.tensor_scalar(xg[:, s % 2, f, :], x[:, f * P:(f + 1) * P],
                                          bflat[:, bass.ds(i * 16 + (2 * s + f), 1)], 7.0, ALU.add, ALU.min)
                    for f in range(2):
                        j = dve.tensor_scalar(lin[:, s % 2, f, :], x[:, (2 + f) * P:(3 + f) * P],
                                              bflat[:, bass.ds(i * 16 + (8 + 2 * s + f), 1)], 7.0, ALU.add, ALU.min)
                    j.then_inc(dve_took, 1)
                    dve.drain()
                    if s == 0:
                        for t in range(TT):
                            dve.tensor_scalar(S[:, t, :], iota, rflat[:, bass.ds(i + (t * 66 + 1), 1)], None, ALU.is_equal)
                            dve.tensor_scalar(SG[:, t, :], iota, rflat[:, bass.ds(i + t * 66, 1)],
                                              gflat[:, bass.ds(i + t * 66, 1)], ALU.is_equal, ALU.mult)
                        dve.drain().then_inc(S_ready, 1)
                    dve.tensor_scalar(lin[:, s % 2], lin[:, s % 2], -7.0, 1.0, ALU.max, ALU.add)
                    dve.drain()
                    dve.tensor_tensor(lin[:, s % 2], lin[:, s % 2], xg[:, s % 2], ALU.mult)
                    dve.drain()
                    dve.wait_ge(sig_ready, i * 4 + (s + 1))
                    dve.tensor_tensor(actT[:, 2 * s:2 * s + 2, :], lin[:, s % 2], sgm[:, s % 2], ALU.mult).then_inc(act_ready, 1)
            dve.wait_ge(moe_done, 1)
            for t in range(TT):
                dve.tensor_copy(acc[:, t, :].rearrange("p (a b) -> p a b", a=2), psum[:, 4 + 2 * t:6 + 2 * t, :])
            dve.drain()
            spread(4, rf)
            scales(10, acc)
            add_row_scaled(acc, hs)

        @block.gpsimd
        def _(pool):
            pool.wait_ge(hs_ready, 18)
            for i in range(2):
                pool.dma_start(bgu[:, i * E2:(i + 1) * E2], d["bgu"]).then_inc(moe_loaded, 16)
            pool.dma_start(bdn[0:E2, :], d["bdn"]).then_inc(moe_loaded, 16)
            pool.dma_start(wr, d["wr"]).then_inc(moe_loaded, 16)
            pool.dma_start(br[0:1, :], d["br"]).then_inc(moe_loaded, 16)


def _columns(w, width=512):
    k, n = w.shape
    return np.ascontiguousarray(
        w.reshape(k // P, P, n // width, width).transpose(2, 1, 0, 3)).reshape(n // width, P, k // P * width)


def _vec(v):
    return v.reshape(-1, 8, P).transpose(2, 0, 1)


def kernel(**inputs):
    import concourse.bacc as bacc
    from concourse.bass_utils import run_bass_kernel_spmd as run

    a = {k: np.ascontiguousarray(v) for k, v in inputs.items()}
    out = {"x": a["x"]}
    out["small"], out["late"] = constant_tables()
    pairs = [a["norm_mix"], a["kv_norm"][None], a["norm_ffn"], a["norm_ple"], a["final_norm"][None], a["a_conv_w"][0],
             a["a_conv_b"], a["a_b_r"], a["a_b_i"], a["a_lambda"], a["g_pre_mix_2"], a["g_post_mix_2"],
             a["g_pre_ffn_2"], a["g_post_ffn_2"], np.concatenate([a["attn_norm_w_2"], a["hgrn_norm_w_2"]], 1),
             a["c_2"], a["hgrn_lb_2"].reshape(1, D), a["b_ada_2"].reshape(6, D)]
    out["vecs"] = np.ascontiguousarray(_vec(np.concatenate(pairs, 0)))
    out["a_in"] = _columns(a["a_w_in"][0])
    out["a_gates"] = np.ascontiguousarray(
        np.concatenate([a["a_w_r"][0], a["a_w_i"][0]], 0).transpose(1, 0, 2)).reshape(P, 16 * P)
    out["a_out"] = _columns(a["a_w_out"][0])
    out["peer_wq"] = np.stack([_columns(w) for w in a["peer_w_q"]])
    out["keys"] = np.ascontiguousarray(
        a["peer_sub_keys"].reshape(2, 16, NK, P).transpose(0, 3, 1, 2)).reshape(2, P, 16 * NK)
    out["peer_u"] = np.ascontiguousarray(
        a["peer_u"].reshape(2, P, 32, 4, KC, P).transpose(0, 2, 5, 4, 3, 1)).reshape(2, 32, P, SLOT)
    out["peer_v"] = np.ascontiguousarray(
        a["peer_v"].reshape(2, P, 32, SLOT).transpose(0, 2, 1, 3))
    out["ple_gate"] = np.stack([_columns(w) for w in a["ple_w_gate"]])
    out["ple_proj"] = np.ascontiguousarray(
        a["ple_w_proj"].reshape(2, 2, P, D).transpose(0, 2, 1, 3)).reshape(2, P, 2 * D)
    out["pT"] = np.ascontiguousarray(a["p"].reshape(2, T, 2, P).transpose(0, 3, 2, 1))
    out["kv"] = _columns(a["w_kv"])
    out["bq"] = _columns(a["b_w_q"][0])
    out["bo"] = _columns(a["b_w_o"][0])
    out["ada"] = _columns(a["w_ada_2"][0])
    out["mix_in"] = _columns(a["w_in_2"][0])
    out["mix_out"] = _columns(a["w_out_2"][0])
    moe = np.empty((E2, 6, P, KC, 512), np.float32)
    moe[:, 0:4] = a["w_gu_2"][0].reshape(E2, KC, P, 2, 4, 256).transpose(0, 4, 2, 1, 3, 5).reshape(E2, 4, P, KC, 512)
    moe[:, 4:6] = a["w_down_2"][0].reshape(E2, KC, P, 2, 512).transpose(0, 3, 2, 1, 4)
    out["moe"] = moe.reshape(E2, 6, P, SLOT)
    out["bgu"] = np.ascontiguousarray(a["b_gu_2"][0].reshape(E2, 16, P).transpose(2, 0, 1))
    out["bdn"] = a["b_down_2"][0]
    out["wr"] = np.ascontiguousarray(a["w_router_2"][0].reshape(KC, P, E2).transpose(1, 0, 2))
    out["br"] = a["b_router_2"]

    nc = bacc.Bacc("TRN2", target_bir_lowering=False, num_devices=1)
    d = {k: nc.dram_tensor(f"in_{k}", v.shape, F32, kind="ExternalInput").ap() for k, v in out.items()}
    d["out"] = nc.dram_tensor("out_0", (1, T, D), F32, kind="ExternalOutput").ap()
    build(nc, d)
    r = run(nc, [{f"in_{k}": v for k, v in out.items()}], core_ids=[0])
    return r.results[0]["out_0"]
```

```python
from contextlib import ExitStack

import numpy as np
import concourse.bass as bass
from concourse import mybir

F32 = mybir.dt.float32
F32R = mybir.dt.float32r
U32 = mybir.dt.uint32
I32 = mybir.dt.int32
ALU = mybir.AluOpType
ACT = mybir.ActivationFunctionType
AX = mybir.AxisListType

P = 128
T = 256
TT = T // P
D = 1024
KC = D // P
EPS = 1e-6
HEADS = 16
PH = 8
NK = 128
TOPK = 16
E2 = 32
DIL_HEADS = 8
REC_HEADS = 4
CHUNK = 32
RING = 2
UNIT = 512
UNITS = 8
PARTS = 3
SLOT = 4096
NEG = -3.0e38
SC = 0.125

STREAM = (
    ("a_in", 4, "AA"), ("a_gates", 1, "A" * 8), ("a_out", 2, "DD"),
    ("peer_q0", 4, "AA"), ("peer_keys0", 1, "A" * 8), ("peer_u0", 32, "AA"), ("peer_v0", 32, "--"),
    ("ple_gate0", 2, "AA"), ("ple_proj0", 1, "DDDD"),
    ("kv", 4, "AA"), ("bq", 2, "AA"), ("bo", 2, "DD"),
    ("peer_q1", 4, "AA"), ("peer_keys1", 1, "A" * 8), ("peer_u1", 32, "AA"), ("peer_v1", 32, "--"),
    ("ple_gate1", 2, "AA"), ("ple_proj1", 1, "DDDD"),
    ("ada", 12, "D"), ("mix_in", 7, ("AA", "AA", "AA", "DD", "AA", "AA", "DD")), ("mix_out", 2, "DD"),
    ("moe", 6, ("D", "D", "D", "DAAA", "A", "A")),
)
BLOCK_TILES = 9


def stream_plan():
    first, ends, engine, nth, unit = {}, [], [], [], {}
    count = {"A": 0, "D": 0, "-": 0}
    for stage, slots, who in STREAM:
        first[stage] = len(ends)
        if stage.startswith(("peer_u", "peer_v")):
            unit[stage] = UNITS * 32 * len(unit)
        for s in range(slots):
            for e in (who[s] if isinstance(who, tuple) else who):
                count[e] += 1
                engine.append(e)
                nth.append(count[e])
            ends.append(len(engine))
    return first, ends, engine, nth, unit


VECS = ("norm_mix0", "norm_mix1", "kv_norm", "norm_ffn0", "norm_ffn1", "norm_ple0", "norm_ple1", "final_norm",
        "conv0", "conv1", "conv2", "conv3", "conv_b", "b_r", "b_i", "lam",
        "g_pre_mix", "g_post_mix", "g_pre_ffn", "g_post_ffn", "mix_norm", "c", "lb",
        "ada0", "ada1", "ada2", "ada3", "ada4", "ada5")
V = {n: i for i, n in enumerate(VECS)}

C_MASK, C_TRI, C_ONES, C_NEG, C_CNT, C_REC, C_RESET = 0, 384, 512, 640, 1024, 1408, 1536
C_IOTA32, C_END = 1792, 1824


def constant_tables():
    k = np.arange(P)[:, None]
    q = np.arange(P)[None, :]
    one = np.ones((P, P), np.float32)
    strict = (k < q).astype(np.float32)
    mask = np.concatenate([strict, one, strict], 1)
    tri = (k > q).astype(np.float32)
    def count(q0, k0):
        d = (q0 + k) - (k0 + q)
        n = ((d >= 0) & (d <= 128)).astype(np.float32)
        n += ((d >= 0) & (d % 4 == 0) & (d <= 512))
        n += ((d >= 0) & (d % 16 == 0) & (d <= 2048))
        return n.astype(np.float32)
    cnt = np.concatenate([count(0, 0), count(128, 0), count(128, 128)], 1)
    neg = np.where(cnt > 0, 0.0, -1e30).astype(np.float32)
    rec = ((k // CHUNK == q // CHUNK) & (k <= q)).astype(np.float32)
    reset = np.tile((np.arange(T) % CHUNK != 0).astype(np.float32), (P, 1))
    iota = np.tile(np.arange(32, dtype=np.float32), (P, 1))
    small = np.concatenate([np.eye(P, dtype=np.float32), np.tile(np.arange(P, dtype=np.float32), (P, 1))], 1)
    late = np.concatenate([mask, tri, one, neg, cnt, rec, reset, iota], 1)
    assert late.shape[1] == C_END
    return small, late


def build(nc, d):
    FIRST, ENDS, TILE_ENGINE, TILE_NTH, FIRST_UNIT = stream_plan()
    SPLIT = {FIRST[k] + s: FIRST_UNIT[k] + UNITS * s for k in FIRST_UNIT for s in range(32)}

    def tile0(stage):
        s = FIRST[stage]
        return ENDS[s - 1] if s else 0

    with ExitStack() as ctx:
        def sb(name, shape, dt=F32):
            return ctx.enter_context(nc.sbuf_tensor(name, shape, dt))

        def sem(name):
            return ctx.enter_context(nc.semaphore(name))

        ring = sb("ring", [P, RING, SLOT])
        big = sb("big", [P, 32768])
        def region(at, *shape):
            n = int(np.prod(shape))
            v = big[:, at:at + n]
            if len(shape) == 2:
                return v.rearrange("p (a b) -> p a b", a=shape[0])
            if len(shape) == 3:
                return v.rearrange("p (a b c) -> p a b c", a=shape[0], b=shape[1])
            return v

        h = sb("h", [P, TT, D])
        xT = region(20480, KC, T)
        whi = sb("whi", [P, PARTS, UNIT], F32R)
        wlo = sb("wlo", [P, PARTS, UNIT], F32R)
        xhi = sb("xhi", [P, KC * T], F32R)
        xlo = sb("xlo", [P, KC * T], F32R)
        zero = sb("zero", [P, P])
        small = sb("small", [P, 2 * P])
        ident = small[:, 0:P]
        iota = small[:, P:2 * P]
        vecs = sb("vecs", [P, len(VECS), 8])
        ss = sb("ss", [P, 2])
        ms = sb("ms", [P, 2])
        std = sb("std", [P, 2])
        rstd = sb("rstd", [P, 2])
        pick = sb("pick", [P, 3, TT, P])
        scratch = sb("scratch", [P, 3 * T])
        pickT = scratch[:].rearrange("p (a b) -> p a b", a=3)
        cval = sb("cval", [P, TT, PH, TOPK])
        sv = sb("sv", [P, 2, TOPK])
        si = sb("si", [P, 2, TOPK], U32)
        sif = sb("sif", [P, 2, TOPK])
        keys_in = scratch[:, 0:T].rearrange("p (a b) -> p a b", a=2)
        work = scratch[:, T:2 * T].rearrange("p (a b) -> p a b", a=TOPK)
        cand = scratch[:, 2 * T:3 * T].rearrange("p (a b) -> p a b", a=TOPK)
        cv = sb("cv", [P, TOPK])
        ci = sb("ci", [P, TOPK], U32)
        cab = sb("cab", [P, 2, TOPK], U32)
        cabf = sb("cabf", [P, 2, TOPK])
        tiny = sb("tiny", [P, 16, 8])
        psum = ctx.enter_context(nc.psum_tensor("psum", [P, 8, 512], F32))

        def V8(name):
            return vecs[:, V[name], :]

        hs = region(0, TT, D)

        acts = region(0, NK, T)
        scores = region(112 * T, TT, 16, NK)
        qT = region(96 * T, 16, T)
        xh3, xl3 = (v[:].rearrange("p (k t) -> p k t", k=KC) for v in (xhi, xlo))
        away, away2, hot1 = (v.rearrange("p (b k n) -> p b k n", b=2, k=4) for v in (
            xhi[:, 0:1024], xhi[:, 1024:2048], xlo[:, 0:1024]))

        def hot2(b, k):
            n = 4 * b + k
            if n < 6:
                return pick[:, n // 2, n % 2, :]
            return cval[:, n - 6].rearrange("p a b -> p (a b)")

        vhi, vlo = (v[:].rearrange("p (b c) -> p b c", b=2) for v in (xhi, xlo))

        gy = region(2048, KC, T)
        xb = region(4096, KC, T + 3)
        xc = region(4096 + KC * (T + 3), KC, T)
        lru = [region(8448 + 2048 * i, KC, T) for i in range(6)]

        gate_sb = region(2048, TT, D)
        ple_t = region(4096, TT, D)
        pT = region(6144, 2, T)

        xT2 = region(2048, KC, T)
        kT = region(4096, KC, T)
        qbT = region(6144, KC, T)
        v_sb = region(8192, TT, D)
        oT = region(10240, KC, T)
        late = region(12288, C_END)
        w_sb = region(14336, HEADS, 384)
        lm = region(20480, HEADS, 384)
        za = region(26624, 3, 2, 384)
        zl = region(28928, 2, 384)

        row = region(2048, D)
        diag = region(3072, KC, P)
        modv = sb("modv", [P, 48])
        mod_row = region(4096, 6 * D)
        qaT = region(4096, 4, T)
        kaT = region(5120, 4, T)
        va = region(6144, TT, 512)
        qrT = region(7168, 4, T)
        frT = region(8192, 4, T)
        vr = region(9216, TT, 512)
        gr = region(10240, TT, 512)
        ylow = region(16384, TT, D)
        sm = region(18432, 2, 384)
        em = region(19200, 2, 384)
        pmT = region(19968, 2, 384)
        dnum = region(20736, 8, 4)
        sq = region(20768, TT, D)
        hst = region(22816, 24)
        f_ = region(24576, 4, T)
        b_ = region(25600, 4, T)
        eb = region(26624, 4, T)
        qe = region(27648, 4, T)
        ke = region(28672, 4, T)
        kd = region(29696, 4, T)
        kdt = region(30720, 4, TT, P)
        am = region(22912, 4, TT, P)
        states = region(14336, 4, 4, P)
        blast = region(31744, 4, 8)
        decay = region(31776, 4, 8)
        ysb = region(18432, TT, D)

        bgu = region(4096, 2 * E2, 16)
        bdn = region(5120, D)
        wr = region(6144, KC, E2)
        br = region(6400, E2)
        rank = region(6464, TT, 66)
        G2 = region(6600, TT, 66)
        member = region(6740, TT, E2)
        G = region(6820, TT, E2)
        logit = region(6890, TT, E2)
        gT = region(6960, T)
        tk = region(7220, 64)
        tki = region(7290, 16).bitcast(U32)
        most = region(7310, E2)
        blocks = region(7350, 1).bitcast(I32)
        actT = region(8192, KC, P)
        xgT = region(9216, KC, P)
        S = region(10240, TT, P)
        SG = region(10496, TT, P)
        SGT = region(10752, T)
        Y = region(11008, D)
        xg = region(14336, 2, 2, P)
        sgm = region(14848, 2, 2, P)
        lin = region(15360, 2, 2, P)
        row2 = region(16384, D)
        acc = region(18432, TT, D)

        loaded = [sem(f"half_loaded{i}") for i in range(2 * RING)]
        half_done = sem("half_done")
        hi_ready = sem("hi_ready")
        lo_ready, pool_lo_ready = sem("lo_ready"), sem("pool_lo_ready")
        part_room = sem("part_room")
        xhi_ready, xlo_ready, vhi_ready, vlo_ready = sem("xhi_ready"), sem("xlo_ready"), sem("vhi_ready"), sem("vlo_ready")
        away_ready, hot1_ready = sem("away_ready"), sem("hot1_ready")
        tile_done = sem("tile_done")
        act_took = sem("act_took")
        dve_took = sem("dve_took")
        x_loaded = sem("x_loaded")
        small_loaded = sem("small_loaded")
        var_ready, std_ready, hs_ready = sem("var_ready"), sem("std_ready"), sem("hs_ready")
        turned, xT_ready = sem("turned"), sem("xT_ready")
        pads_ready, conv_ready, spl_ready = sem("pads_ready"), sem("conv_ready"), sem("spl_ready")
        expl_ready = sem("expl_ready")
        tanh_ready, sqrt_ready, gated_ready = sem("tanh_ready"), sem("sqrt_ready"), sem("gated_ready")
        topk_done, gexp_in, gexp_out = sem("topk_done"), sem("gexp_in"), sem("gexp_out")
        pick_ready, pick_turned, pickT_ready = sem("pick_ready"), sem("pick_turned"), sem("pickT_ready")
        hot_ready, wmat_done, gated_acts = sem("hot_ready"), sem("wmat_done"), sem("gated_acts")
        zero_ready = sem("zero_ready")
        p_loaded, late_loaded = sem("p_loaded"), sem("late_loaded")
        z_done, zabs_ready, zlog_ready, lm_ready = sem("z_done"), sem("zabs_ready"), sem("zlog_ready"), sem("lm_ready")
        suffix_done, aexp_in, aexp_out, a_ready = sem("suffix_done"), sem("aexp_in"), sem("aexp_out"), sem("a_ready")
        o_done, o_taken = sem("o_done"), sem("o_taken")
        cond_sig, cond_ready, diag_ready, row_done, row_taken = (
            sem("cond_sig"), sem("cond_ready"), sem("diag_ready"), sem("row_done"), sem("row_taken"))
        mod_turned = sem("mod_turned")
        silu_sig, silu_taken = sem("silu_sig"), sem("silu_taken")
        da_done, da_in, da_exp, da_p, da_turned, da_copied, da_o, da_taken = [sem(f"dil_{n}") for n in (
            "scores", "max", "exp", "probs", "turned", "copied", "out", "taken")]
        lb_in, lb_sig, f_ready, logf_ready, b_ready, eb_ready, kd_ready = [sem(f"rec_{n}") for n in (
            "lb_in", "lb_sig", "f", "logf", "b", "exp", "kd")]
        kdt_done, kdt_taken, am_done, am_taken, delta_done, state_ready, ro_done = [sem(f"rec_{n}") for n in (
            "kdt_done", "kdt_taken", "am_done", "am_taken", "delta_done", "state", "out")]
        moe_loaded, logits_done, gexp2_in, gexp2_out, g_ready, gT_done, gT_ready, bd_done, act_ready, sig_ready = [
            sem(f"moe_{n}") for n in ("loaded", "logits", "exp_in", "exp_out", "gates", "gates_turned", "gatesT",
                                      "bias_out", "act", "sigmoid")]
        blocks_ready, first_S, gather0_done, gather0_taken, S_ready, moe_done = [sem(f"moe_{n}") for n in (
            "blocks", "first_onehot", "gather0_done", "gather0_taken", "onehot", "done")]
        member_ready, ranks_done = sem("moe_member"), sem("moe_ranks")
        y_ready, out_stored = sem("y_ready"), sem("out_stored")

        block = ctx.enter_context(nc.Block())

        @block.sync
        def _(sp):
            sp.dma_start(h[:], d["x"][0].rearrange("(a p) d -> p a d", p=P)).then_inc(x_loaded, 16)

            def half(n, f, src, words=SLOT):
                at = f * words // 2
                sp.dma_start(ring[:, n % RING, at:at + words // 2], src[:, at:at + words // 2]).then_inc(
                    loaded[2 * (n % RING) + f], 16)

            def load(n, src, words=SLOT):
                b = n - RING
                for f in range(2):
                    if b in SPLIT:
                        sp.wait_ge(part_room, SPLIT[b] + UNITS // 2 * (f + 1) + PARTS - 1)
                    elif b >= 0 and f == 0:
                        sp.wait_ge(tile_done, ENDS[b])
                    half(n, f, src, words)

            def plain(stage, w):
                for s in range(w.shape[0]):
                    load(FIRST[stage] + s, w[s])

            def experts(stage, w):
                n0, u0 = FIRST[stage], FIRST_UNIT[stage]
                for s in range(RING):
                    load(n0 + s, w[s])
                with sp.Fori(0, 5) as i:
                    for s in range(6):
                        for f in range(2):
                            sp.wait_ge(part_room, i * 48 + (u0 + UNITS * s + UNITS // 2 * (f + 1) + PARTS - 1))
                            half(n0 + s, f, w[i * 6 + (s + RING)])

            def peer(l):
                plain(f"peer_q{l}", d["peer_wq"][l])
                load(FIRST[f"peer_keys{l}"], d["keys"][l], words=16 * NK)
                experts(f"peer_u{l}", d["peer_u"][l])
                experts(f"peer_v{l}", d["peer_v"][l])
                plain(f"ple_gate{l}", d["ple_gate"][l])
                load(FIRST[f"ple_proj{l}"], d["ple_proj"][l], words=2 * D)

            plain("a_in", d["a_in"])
            load(FIRST["a_gates"], d["a_gates"], words=16 * P)
            plain("a_out", d["a_out"])
            peer(0)
            plain("kv", d["kv"])
            plain("bq", d["bq"])
            plain("bo", d["bo"])
            peer(1)
            plain("ada", d["ada"])
            plain("mix_in", d["mix_in"])
            plain("mix_out", d["mix_out"])
            n0 = FIRST["moe"]
            w = d["moe"]
            for s in range(RING):
                load(n0 + s, w[0, s])
            sp.wait_ge(blocks_ready, 1)
            n = sp.value_load(blocks[0:1, 0:1], min_val=E2, max_val=2 * E2)

            def turn_of(s, i, src):
                sp.wait_ge(half_done, i * 6 + (s + 7))
                half(n0 + s, 0, src)
                sp.wait_ge(tile_done, i * BLOCK_TILES + ENDS[n0 + s])
                half(n0 + s, 1, src)

            with sp.Fori(0, n - 1) as i:
                for s in range(4):
                    turn_of(s, i, w[i % E2, s + 2])
                for s in range(4, 6):
                    turn_of(s, i, w[(i + 1) % E2, s - 4])
            for s in range(4):
                turn_of(s, n - 1, w[E2 - 1, s + 2])
            sp.wait_ge(y_ready, TT)
            sp.dma_start(d["out"][0].rearrange("(a p) d -> p a d", p=P), hs).then_inc(out_stored, 16)
            sp.wait_ge(out_stored, 16)

        @block.tensor
        def _(pe):
            def slot_in(n, extra=0, halves=(0, 1)):
                for f in halves:
                    pe.wait_ge(loaded[2 * (n % RING) + f], extra + 16 * (n // RING + 1))
                return ring[:, n % RING, :]

            def bank_free(m):
                if m >= 3 and TILE_ENGINE[m - 3] != "-":
                    pe.wait_ge(act_took if TILE_ENGINE[m - 3] == "A" else dve_took, TILE_NTH[m - 3])

            def features(stage, s, rhs, free=bank_free, extra=0, n=None):
                n = FIRST[stage] + s if n is None else n
                w = slot_in(n, extra).rearrange("p (k f) -> p k f", k=KC)
                m = ENDS[n] - 2
                for t in range(2):
                    free(m + t)
                    for f in range(2):
                        c = (2 * t + f) * P
                        for k in range(KC):
                            mm = pe.matmul(psum[:, (m + t) % 3, f * T:(f + 1) * T], w[:, k, c:c + P], rhs[:, k, :],
                                           start=(k == 0), stop=(k == KC - 1))
                    mm.then_inc(tile_done, 1)

            def tokens(stage, s, lhs, free=bank_free, extra=0, n=None):
                n = FIRST[stage] + s if n is None else n
                w = slot_in(n, extra).rearrange("p (k f) -> p k f", k=KC)
                m = ENDS[n] - 2
                for t in range(TT):
                    free(m + t)
                    for k in range(KC):
                        mm = pe.matmul(psum[:, (m + t) % 3, :], lhs[:, k, t * P:(t + 1) * P], w[:, k, :],
                                       start=(k == 0), stop=(k == KC - 1))
                    mm.then_inc(tile_done, 1)

            def turn(i, src=hs):
                pe.wait_ge(hs_ready, 2 * (i + 1))
                for b in range(4):
                    for k in range(2):
                        for t in range(TT):
                            c = (2 * b + k) * P
                            mm = pe.transpose(psum[:, 4 + b, k * T + t * P:k * T + (t + 1) * P],
                                              src[:, t, c:c + P], ident)
                    mm.then_inc(turned, 1)

            def unit(j, it=None):
                if j % 3 == 2:
                    pe.wait_ge(pool_lo_ready, (0 if it is None else it * 16) + (j + 1) // 3)
                else:
                    pe.wait_ge(lo_ready, (0 if it is None else it * 32) + (j + 1 - (j + 1) // 3))
                return whi[:, j % PARTS, :], wlo[:, j % PARTS, :]

            pe.sem_inc(part_room, 2)
            pe.sem_inc(half_done, 6)
            pe.wait_ge(small_loaded, 32)
            turn(0)
            pe.wait_ge(xT_ready, 4)
            for s in range(4):
                features("a_in", s, xT)
            w = slot_in(FIRST["a_gates"])
            m = tile0("a_gates")
            for g in range(8):
                pe.wait_ge(conv_ready, min(2 * (g % 4) + 2, 8))
                bank_free(m + g)
                for f in range(2):
                    j = 2 * g + f
                    mm = pe.matmul(psum[:, (m + g) % 3, f * T:(f + 1) * T], w[:, j * P:(j + 1) * P],
                                   xc[:, j % 8, :], start=True, stop=True)
                mm.then_inc(tile_done, 1)
            pe.wait_ge(gated_ready, 1)
            for s in range(2):
                tokens("a_out", s, lru[5])

            def peer(l, i):
                turn(i)
                pe.wait_ge(xT_ready, 4 * (i + 1) + 4 * l)
                for s in range(4):
                    features(f"peer_q{l}", s, xT)
                w = slot_in(FIRST[f"peer_keys{l}"])
                m = tile0(f"peer_keys{l}")
                pe.wait_ge(act_took, TILE_NTH[m - 1])
                for g in range(8):
                    bank_free(m + g)
                    for f in range(4):
                        j = 4 * (g % 4) + f
                        mm = pe.matmul(psum[:, (m + g) % 3, f * P:(f + 1) * P], qT[:, j, (g // 4) * P:(g // 4 + 1) * P],
                                       w[:, j * NK:(j + 1) * NK], start=True, stop=True)
                    mm.then_inc(tile_done, 1)
                m0, u0 = tile0(f"peer_u{l}"), FIRST_UNIT[f"peer_u{l}"]
                pe.wait_ge(xlo_ready, l + 1)

                def u_slots(slots, it=None):
                    for s in range(slots):
                        for t in range(2):
                            m = m0 + 2 * s + t
                            pe.wait_ge(act_took, (0 if it is None else it * 12) + TILE_NTH[m - 3])
                            for f in range(2):
                                o = psum[:, m % 3, f * T:(f + 1) * T]
                                for c in range(2):
                                    j = u0 + UNITS * s + 4 * t + 2 * f + c
                                    hi, lo = unit(j, it)
                                    for k in range(4):
                                        w = slice(k * P, (k + 1) * P)
                                        mm = pe.matmul(o, hi[:, w], xh3[:, 4 * c + k, :], start=(c + k == 0), stop=False)
                                        if k == 0:
                                            mm.then_inc(part_room, 1)
                                        pe.matmul(o, hi[:, w], xl3[:, 4 * c + k, :], start=False, stop=False)
                                        mm = pe.matmul(o, lo[:, w], xh3[:, 4 * c + k, :], start=False,
                                                       stop=(c == 1 and k == 3))
                            mm.then_inc(tile_done, 1)

                with pe.Fori(0, 5) as it:
                    u_slots(6, it)
                m0, u0 = m0 + 60, u0 + 240
                u_slots(2)
                pe.wait_ge(pick_ready, l + 1)
                for r in range(3):
                    for t in range(TT):
                        c = (r % 2) * T + t * P
                        mm = pe.transpose(psum[:, 4 + r // 2, c:c + P], pick[:, r, t, :], ident)
                mm.then_inc(pick_turned, 1)
                with pe.Fori(0, 16) as it:
                    for g in range(4):
                        pe.wait_ge(hot1_ready, it * 4 + (64 * l + g + 1))
                        pe.wait_ge(hot_ready, it * 4 + (64 * l + g + 1))
                        for k in range(4):
                            o = psum[:, 4 + g, k * P:(k + 1) * P]
                            mm = pe.matmul(o, hot1[:, g % 2, k, :].bitcast(F32), hot2(g % 2, k), start=True, stop=True)
                        mm.then_inc(wmat_done, 1)
                u0 = FIRST_UNIT[f"peer_v{l}"]
                pe.wait_ge(vlo_ready, 32 * l + 1)
                pe.wait_ge(zero_ready, 1)
                for b in range(4):
                    pe.matmul(psum[:, 4 + b, :], zero[:], h[:, 0, 0:512], start=True, stop=False, skip_group_check=True)

                def v_slots(slots, s0, it=None, last=False):
                    for s in range(slots):
                        pe.wait_ge(vlo_ready, (0 if it is None else it * 6) + (32 * l + s0 + s + 1))
                        for q in range(UNITS):
                            e, c = q // 2, q % 2
                            hi, lo = unit(u0 + UNITS * (s0 + s) + q, it)
                            for t in range(TT):
                                x = slice(e * T + t * P, e * T + (t + 1) * P)
                                o = psum[:, 4 + 2 * t + c, :]
                                end = last and s == slots - 1 and e == 3
                                mm = pe.matmul(o, vhi[:, s % 2, x], hi, start=False, stop=False, skip_group_check=True)
                                if t == 0:
                                    mm.then_inc(part_room, 1)
                                pe.matmul(o, vlo[:, s % 2, x], hi, start=False, stop=False, skip_group_check=True)
                                mm = pe.matmul(o, vhi[:, s % 2, x], lo, start=False, stop=end, skip_group_check=True)
                            if q % 4 == 3:
                                mm.then_inc(tile_done, 1)

                with pe.Fori(0, 5) as it:
                    v_slots(6, 0, it)
                v_slots(2, 30, last=True)

            def ple(l, i):
                turn(i)
                pe.wait_ge(xT_ready, 4 * (i + 1) + 4 * l)
                for s in range(2):
                    tokens(f"ple_gate{l}", s, xT)
                pe.wait_ge(p_loaded, 16 * (l + 1))
                w = slot_in(FIRST[f"ple_proj{l}"])[:, 0:2 * D].rearrange("p (k f) -> p k f", k=2)
                m = tile0(f"ple_proj{l}")
                for g in range(4):
                    bank_free(m + g)
                    for k in range(2):
                        mm = pe.matmul(psum[:, (m + g) % 3, :], pT[:, k, (g // 2) * P:(g // 2 + 1) * P],
                                       w[:, k, (g % 2) * 512:(g % 2 + 1) * 512], start=(k == 0), stop=(k == 1))
                    mm.then_inc(tile_done, 1)

            peer(0, 1)
            ple(0, 2)

            turn(3)
            pe.wait_ge(xT_ready, 20)
            for s in range(2):
                features("kv", s, xT)
            for s in range(2, 4):
                tokens("kv", s, xT)
            for s in range(2):
                features("bq", s, xT2)
            pe.wait_ge(act_took, TILE_NTH[tile0("bo") - 1])
            pe.wait_ge(late_loaded, 16)
            for a in range(HEADS):
                if a >= 4:
                    pe.wait_ge(lm_ready, a - 3)
                r = slice(64 * (a % 2), 64 * (a % 2) + 64)
                z = psum[:, 4 + a % 4, 0:384]
                pe.matmul(z[:, 0:256], kT[r, a // 2, 0:128], qbT[r, a // 2, :], start=True, stop=True)
                pe.matmul(z[:, 256:384], kT[r, a // 2, 128:256], qbT[r, a // 2, 128:256], start=True, stop=True,
                          ).then_inc(z_done, 1)
            tri, ones = late[:, C_TRI:C_TRI + P], late[:, C_ONES:C_ONES + P]
            for a in range(HEADS):
                pe.wait_ge(lm_ready, min(a + 13, HEADS))
                if a >= 4:
                    pe.wait_ge(aexp_in, a - 3)
                z = psum[:, 4 + a % 4, 0:384]
                pe.matmul(z[:, 128:256], ones, lm[:, a, 256:384], start=True, stop=False, skip_group_check=True)
                pe.matmul(z, tri, lm[:, a, :], start=False, stop=True, skip_group_check=True).then_inc(suffix_done, 1)
            for c in range(HEADS // 2):
                pe.wait_ge(a_ready, 2 * c + 2)
                if c >= 4:
                    pe.wait_ge(o_taken, c - 3)
                else:
                    pe.wait_ge(aexp_in, HEADS)
                for s in range(2):
                    a = 2 * c + s
                    o = psum[64 * s:64 * s + 64, 4 + c % 4, 0:256]
                    pe.matmul(o[:, 128:256], v_sb[:, 1, a * 64:a * 64 + 64], w_sb[:, a, 256:384],
                              start=True, stop=False, skip_group_check=True)
                    mm = pe.matmul(o, v_sb[:, 0, a * 64:a * 64 + 64], w_sb[:, a, 0:256],
                                   start=False, stop=True, skip_group_check=True)
                mm.then_inc(o_done, 1)
            pe.wait_ge(o_taken, HEADS // 2)
            for s in range(2):
                tokens("bo", s, oT)

            peer(1, 4)
            ple(1, 5)

            def spread(i):
                pe.wait_ge(diag_ready, i + 1)
                for k in range(KC):
                    mm = pe.matmul(psum[:, 4 + k // 4, (k % 4) * P:(k % 4 + 1) * P], late[:, C_ONES:C_ONES + P],
                                   diag[:, k, :], start=True, stop=True)
                mm.then_inc(row_done, 1)

            pe.wait_ge(late_loaded, 32)
            spread(0)
            pe.wait_ge(cond_ready, 1)

            def turn_mod(s):
                pe.wait_ge(dve_took, TILE_NTH[tile0("ada") + s])
                for j in range(4 * s, 4 * s + 4):
                    mm = pe.matmul(psum[:, 3, j:j + 1], mod_row[0:1, j * P:(j + 1) * P], ident[0:1, 0:1],
                                   start=True, stop=True)
                return mm

            for s in range(12):
                n = FIRST["ada"] + s
                m = ENDS[n] - 1
                bank_free(m)
                for k in range(KC):
                    if k % 4 == 0:
                        w = slot_in(n, halves=(k // 4,)).rearrange("p (k f) -> p k f", k=KC)
                    mm = pe.matmul(psum[0:1, m % 3, :], tiny[:, 0, k:k + 1], w[:, k, :], start=(k == 0), stop=(k == KC - 1))
                mm.then_inc(tile_done, 1)
                if s:
                    turn_mod(s - 1)
            turn_mod(11).then_inc(mod_turned, 1)
            turn(6)
            pe.wait_ge(xT_ready, 32)
            for s in range(7):
                (features if s in (0, 1, 3, 4) else tokens)("mix_in", s, xT)

            pe.wait_ge(act_took, TILE_NTH[tile0("mix_in") + 5])

            def dil_scores(a):
                if a >= 2:
                    pe.wait_ge(da_in, a - 1)
                r = slice(64 * (a % 2), 64 * (a % 2) + 64)
                z = psum[:, 4 + a % 2, 0:384]
                pe.matmul(z[:, 0:128], qaT[r, a // 2, 0:128], kaT[r, a // 2, 0:128], start=True, stop=True)
                pe.matmul(z[:, 128:384], qaT[r, a // 2, 128:256], kaT[r, a // 2, :], start=True, stop=True,
                          ).then_inc(da_done, 1)

            dil_scores(0)
            for a in range(DIL_HEADS):
                if a + 1 < DIL_HEADS:
                    dil_scores(a + 1)
                pe.wait_ge(da_p, a + 1)
                for j in range(3):
                    mm = pe.transpose(psum[:, 6, j * P:(j + 1) * P], em[:, a % 2, j * P:(j + 1) * P], ident)
                mm.then_inc(da_turned, 1)
                pe.wait_ge(da_copied, a + 1)
                if a:
                    pe.wait_ge(da_taken, a)
                c = slice(a * 64, a * 64 + 64)
                pe.matmul(psum[:, 7, 0:64], pmT[:, a % 2, 0:128], va[:, 0, c], start=True, stop=True)
                pe.matmul(psum[:, 7, 64:128], pmT[:, a % 2, 128:256], va[:, 0, c], start=True, stop=False)
                pe.matmul(psum[:, 7, 64:128], pmT[:, a % 2, 256:384], va[:, 1, c], start=False, stop=True).then_inc(
                    da_o, 1)
            pe.wait_ge(da_taken, DIL_HEADS)

            for a in range(REC_HEADS):
                pe.wait_ge(kd_ready, 3 * a + 3)
                if a:
                    pe.wait_ge(kdt_taken, a)
                for t in range(TT):
                    mm = pe.transpose(psum[:, 4, t * P:(t + 1) * P], kd[:, a, t * P:(t + 1) * P], ident)
                mm.then_inc(kdt_done, 1)
                if a:
                    pe.wait_ge(am_taken, 2 * a)
                for t in range(TT):
                    mm = pe.matmul(psum[:, 5, t * P:(t + 1) * P], ke[:, a, t * P:(t + 1) * P],
                                   qe[:, a, t * P:(t + 1) * P], start=True, stop=True)
                mm.then_inc(am_done, 1)
            pe.wait_ge(kdt_taken, REC_HEADS)
            pe.wait_ge(am_taken, 2 * REC_HEADS)
            for c in range(7):
                if c:
                    pe.wait_ge(state_ready, 4 * c)
                for a in range(REC_HEADS):
                    r = slice(CHUNK * (c % 4), CHUNK * (c % 4) + CHUNK)
                    mm = pe.matmul(psum[:, 4 + c % 2, a * P:(a + 1) * P], kdt[r, a, c // 4, :],
                                   vr[r, c // 4, a * P:(a + 1) * P], start=True, stop=True)
                mm.then_inc(delta_done, 1)
                if c in (2, 6):
                    t = c // 4
                    pe.wait_ge(state_ready, 4 * (c + 1))
                    for a in range(REC_HEADS):
                        o = psum[:, 6 + t, a * P:(a + 1) * P]
                        pe.matmul(o, am[:, a, t, :], vr[:, t, a * P:(a + 1) * P], start=True, stop=False,
                                  skip_group_check=True)
                        for j in range(4):
                            n = 4 * t + j
                            if n:
                                mm = pe.matmul(psum[CHUNK * j:CHUNK * (j + 1), 6 + t, a * P:(a + 1) * P],
                                               qe[:, a, n * CHUNK:(n + 1) * CHUNK], states[:, n % 4, a, :],
                                               start=False, stop=(j == 3), skip_group_check=True)
                    mm.then_inc(ro_done, 1)
            turn(7, ylow)
            pe.wait_ge(xT_ready, 36)
            for s in range(2):
                tokens("mix_out", s, xT)
            spread(1)
            turn(8)
            spread(2)
            spread(3)
            pe.wait_ge(xT_ready, 40)

            pe.wait_ge(moe_loaded, 80)
            for t in range(TT):
                for k in range(KC):
                    pe.matmul(psum[:, 3, t * E2:(t + 1) * E2], xT[:, k, t * P:(t + 1) * P], wr[:, k, :],
                              start=(k == 0), stop=False)
                mm = pe.matmul(psum[:, 3, t * E2:(t + 1) * E2], late[0:1, C_ONES:C_ONES + P], br[0:1, :],
                               start=False, stop=True)
            mm.then_inc(logits_done, 1)
            pe.wait_ge(member_ready, 1)
            strict, ones = late[:, C_MASK:C_MASK + P], late[:, C_ONES:C_ONES + P]
            pe.matmul(psum[:, 3, 0:E2], strict, member[:, 0], start=True, stop=True)
            pe.matmul(psum[:, 3, E2:2 * E2], ones, member[:, 0], start=True, stop=False)
            pe.matmul(psum[:, 3, E2:2 * E2], strict, member[:, 1], start=False, stop=True)
            pe.matmul(psum[:, 3, 2 * E2:3 * E2], ones, member[:, 0], start=True, stop=False)
            pe.matmul(psum[:, 3, 2 * E2:3 * E2], ones, member[:, 1], start=False, stop=True).then_inc(ranks_done, 1)
            for t in range(TT):
                mm = pe.transpose(psum[0:E2, 4, t * P:(t + 1) * P], G[:, t, :], ident)
            mm.then_inc(gT_done, 1)

            def gather(bank):
                for k in range(KC):
                    for t in range(TT):
                        mm = pe.matmul(psum[:, bank(k // 4), (k % 4) * P:(k % 4 + 1) * P], hs[:, t, k * P:(k + 1) * P],
                                       S[:, t, :], start=(t == 0), stop=(t == TT - 1))
                    if k % 4 == 3:
                        yield mm

            pe.wait_ge(first_S, 1)
            for mm in gather(lambda b: 5 + b):
                mm.then_inc(gather0_done, 1)
            pe.wait_ge(gather0_taken, 2)
            for t in range(TT):
                for c in range(2):
                    pe.matmul(psum[:, 4 + 2 * t + c, :], gT[0:E2, t * P:(t + 1) * P],
                              bdn[0:E2, c * 512:(c + 1) * 512], start=True, stop=False, skip_group_check=True)

            def scatter(stop):
                for t in range(TT):
                    for c in range(2):
                        mm = pe.matmul(psum[:, 4 + 2 * t + c, :], SGT[:, t * P:(t + 1) * P], Y[:, c * 512:(c + 1) * 512],
                                       start=False, stop=stop, skip_group_check=True)
                return mm

            n0, m0 = FIRST["moe"], tile0("moe")
            n = pe.value_load(blocks[0:1, 0:1], min_val=E2, max_val=2 * E2)
            with pe.Fori(0, n) as i:
                def free(m):
                    j = m - m0
                    if j < 3:
                        pe.wait_ge(act_took, i * 5 + (TILE_NTH[m + 6] - 5))
                    elif TILE_ENGINE[m - 3] == "A":
                        pe.wait_ge(act_took, i * 5 + TILE_NTH[m - 3])
                    else:
                        pe.wait_ge(dve_took, i * 4 + TILE_NTH[m - 3])

                for s in range(4):
                    free(m0 + s)
                    for f in range(4):
                        if f % 2 == 0:
                            w = slot_in(n0 + s, i * 48, (f // 2,)).rearrange("p (g k f) -> p g k f", g=4, k=KC)
                        for k in range(KC):
                            mm = pe.matmul(psum[:, (m0 + s) % 3, f * P:(f + 1) * P], w[:, f, k, :],
                                           xgT[:, k, :], start=(k == 0), stop=(k == KC - 1))
                        if f == 1:
                            mm.then_inc(half_done, 1)
                    mm.then_inc(tile_done, 1)
                    if s == 0:
                        pe.wait_ge(act_took, i * 5 + (TILE_NTH[m0 + 8] - 5))
                        scatter(False)
                pe.wait_ge(S_ready, i + 1)
                free(m0 + 4)
                for t in range(TT):
                    mm = pe.transpose(psum[:, (m0 + 4) % 3, t * P:(t + 1) * P], SG[:, t, :], ident)
                mm.then_inc(tile_done, 1)
                free(m0 + 5)
                free(m0 + 6)
                for mm in gather(lambda b: (m0 + 5 + b) % 3):
                    mm.then_inc(tile_done, 1)
                pe.wait_ge(act_ready, i * 4 + 4)
                for s in range(4, 6):
                    m = m0 + 3 + s
                    free(m)
                    for k in range(KC):
                        if k % 4 == 0:
                            w = slot_in(n0 + s, i * 48, (k // 4,)).rearrange("p (k f) -> p k f", k=KC)
                        mm = pe.matmul(psum[:, m % 3, :], actT[:, k, :], w[:, k, :], start=(k == 0), stop=(k == KC - 1))
                        if k == 3:
                            mm.then_inc(half_done, 1)
                    mm.then_inc(tile_done, 1)
            pe.wait_ge(act_took, n * 5 + (TILE_NTH[m0 + 8] - 5))
            scatter(True).then_inc(moe_done, 1)
            spread(4)

        @block.scalar
        def _(act):
            act.dma_start(small[:], d["small"]).then_inc(small_loaded, 16)
            act.dma_start(vecs[:], d["vecs"]).then_inc(small_loaded, 16)

            def tile_in(m, plus=0):
                act.wait_ge(tile_done, plus + (m + 1))
                return psum[:, m % 3, :]

            def root(i):
                act.wait_ge(var_ready, i + 1)
                act.activation(std[:], ms[:], ACT.Sqrt).then_inc(std_ready, 1)

            def two(x):
                return x.rearrange("p (a b) -> p a b", a=2)

            def high(j, n, f, it=None):
                plus, extra = (0, 0) if it is None else (it * 48, it * 48)
                if f % 4 == 0:
                    act.wait_ge(loaded[2 * (n % RING) + f // 4], extra + 16 * (n // RING + 1))
                act.wait_ge(part_room, plus + (j + 1))
                act.activation(whi[:, j % PARTS, :], ring[:, n % RING, f * UNIT:(f + 1) * UNIT],
                               ACT.Copy).then_inc(hi_ready, 1)

            act.wait_ge(spl_ready, 1)
            act.activation(tiny[:, 1, :], tiny[:, 0, :], ACT.Exp, scale=-1.0).then_inc(expl_ready, 1)
            root(0)
            m = tile0("a_in")
            for g in range(4):
                act.activation(gy[:, 2 * g:2 * g + 2, :], two(tile_in(m + g)), ACT.Gelu_apprx_tanh).then_inc(act_took, 1)
            act.wait_ge(pads_ready, 1)
            for g in range(4, 8):
                act.activation(xb[:, 2 * g - 8:2 * g - 6, 3:3 + T], two(tile_in(m + g)), ACT.Copy).then_inc(act_took, 1)
            m = tile0("a_gates")
            for g in range(8):
                x = tile_in(m + g)
                for f in range(2):
                    j = 2 * g + f
                    i = act.activation(lru[j // 8][:, j % 8, :], x[:, f * T:(f + 1) * T], ACT.Sigmoid,
                                       bias=V8("b_r" if j < 8 else "b_i")[:, j % 8:j % 8 + 1])
                i.then_inc(act_took, 1)
            act.wait_ge(spl_ready, 2)
            act.drain()
            for a in range(KC):
                i = act.activation(lru[2][:, a, :], lru[0][:, a, :], ACT.Tanh, scale=tiny[:, 6, a:a + 1])
            i.then_inc(tanh_ready, 1)
            act.wait_ge(tanh_ready, 1)
            act.activation(lru[3], lru[2], ACT.Sqrt).then_inc(sqrt_ready, 1)

            def peer(l, i):
                root(i)
                m = tile0(f"peer_q{l}")
                for g in range(8):
                    act.activation(qT[:, 2 * g:2 * g + 2, :], two(tile_in(m + g)), ACT.Copy).then_inc(act_took, 1)
                m = tile0(f"peer_keys{l}")
                for g in range(8):
                    act.activation(scores[:, g // 4, 4 * (g % 4):4 * (g % 4) + 4, :],
                                   tile_in(m + g).rearrange("p (a b) -> p a b", a=4), ACT.Copy).then_inc(act_took, 1)
                act.wait_ge(xT_ready, 4 * (i + 1) + 4 * l)
                act.activation(xhi[:], xT.rearrange("p a b -> p (a b)"), ACT.Copy).then_inc(xhi_ready, 1)
                m, n0, u0 = tile0(f"peer_u{l}"), FIRST[f"peer_u{l}"], FIRST_UNIT[f"peer_u{l}"]
                flat = acts.rearrange("p a b -> p (a b)")
                for j in range(PARTS):
                    high(u0 + j, n0, j)

                def u_slots(slots, s0, it=None):
                    for s in range(s0, s0 + slots):
                        for q in range(UNITS):
                            j = UNITS * s + q + PARTS
                            if j < 256 + PARTS - 1:
                                high(u0 + j, n0 + j // UNITS, j % UNITS, it)
                            if q % 4 == 3:
                                g = 2 * s + q // 4
                                at = g * 512 if it is None else it * (12 * 512) + g * 512
                                x = tile_in(m + g, 0 if it is None else it * 12)
                                act.activation(flat[:, bass.ds(at, 512)], x, ACT.Gelu_apprx_tanh).then_inc(act_took, 1)

                with act.Fori(0, 4) as it:
                    u_slots(6, 0, it)
                act.wait_ge(topk_done, l + 1)
                u_slots(8, 24)
                act.wait_ge(gexp_in, l + 1)
                act.activation(cval[:], cval[:], ACT.Exp).then_inc(gexp_out, 1)
                def one_hot(b, n):
                    act.wait_ge(away_ready, n)
                    act.activation(away2[:, b], away[:, b].bitcast(F32), ACT.Square)
                    act.drain()
                    act.activation(hot1[:, b], away2[:, b].bitcast(F32), ACT.Relu, scale=-1.0, bias=iota[:, 1:2]).then_inc(hot1_ready, 1)

                one_hot(0, 64 * l + 1)
                one_hot(1, 64 * l + 2)
                with act.Fori(0, 31) as it:
                    for b in range(2):
                        act.wait_ge(wmat_done, it * 2 + (64 * l + b + 1))
                        one_hot(b, it * 2 + (64 * l + b + 3))
                act.wait_ge(gated_acts, 64 * (l + 1))
                n0, u0 = FIRST[f"peer_v{l}"], FIRST_UNIT[f"peer_v{l}"]

                def stage(b, at):
                    act.activation(vhi[:, b, :], flat[:, bass.ds(at, D)], ACT.Copy).then_inc(vhi_ready, 1)

                def v_slots(slots, s0, it=None):
                    for s in range(s0, s0 + slots):
                        for q in range(UNITS):
                            j = UNITS * s + q + PARTS
                            if j < 256:
                                high(u0 + j, n0 + j // UNITS, j % UNITS, it)
                            if q == 1 and s < 31:
                                stage((s + 1) % 2, (s + 1) * D if it is None else it * (6 * D) + (s + 1) * D)

                stage(0, 0)
                high(u0 + PARTS - 1, n0, PARTS - 1)
                with act.Fori(0, 5) as it:
                    v_slots(6, 0, it)
                v_slots(2, 30)

            def ple(l, i):
                act.wait_ge(vhi_ready, 32 * (l + 1))
                act.wait_ge(vlo_ready, 32 * (l + 1))
                act.dma_start(pT, d["pT"][l]).then_inc(p_loaded, 16)
                act.dma_start(late, d["late"]).then_inc(late_loaded, 16)
                root(i)
                m = tile0(f"ple_gate{l}")
                for g in range(4):
                    act.activation(gate_sb[:, g % 2, (g // 2) * 512:(g // 2 + 1) * 512], tile_in(m + g),
                                   ACT.Sigmoid).then_inc(act_took, 1)

            peer(0, 1)
            ple(0, 2)

            root(3)
            m = tile0("kv")
            for g in range(4):
                act.activation(kT[:, 2 * g:2 * g + 2, :], two(tile_in(m + g)), ACT.Copy).then_inc(act_took, 1)
            for g in range(4, 8):
                act.activation(v_sb[:, g % 2, (g - 4) // 2 * 512:(g - 4) // 2 * 512 + 512], tile_in(m + g),
                               ACT.Copy).then_inc(act_took, 1)
            m = tile0("bq")
            for g in range(4):
                act.activation(qbT[:, 2 * g:2 * g + 2, :], two(tile_in(m + g)), ACT.Copy).then_inc(act_took, 1)
            for a in range(HEADS):
                act.wait_ge(z_done, a + 1)
                if a >= 2:
                    act.wait_ge(lm_ready, a - 1)
                z = psum[:, 4 + a % 4, 0:384]
                act.activation(za[:, 0, a % 2, :], z, ACT.Abs).then_inc(zabs_ready, 1)
                act.wait_ge(zabs_ready, 2 * a + 1)
                act.activation(za[:, 1, a % 2, :], za[:, 0, a % 2, :], ACT.Exp, scale=-SC).then_inc(zabs_ready, 1)
                act.wait_ge(zabs_ready, 2 * a + 2)
                act.activation(zl[:, a % 2, :], za[:, 1, a % 2, :], ACT.Ln, bias=1.0).then_inc(zlog_ready, 1)
            for a in range(HEADS):
                act.wait_ge(aexp_in, a + 1)
                act.activation(w_sb[:, a, :], w_sb[:, a, :], ACT.Exp).then_inc(aexp_out, 1)
            for c in range(HEADS // 2):
                act.wait_ge(o_done, c + 1)
                act.activation(oT[:, c, :], psum[:, 4 + c % 4, 0:256], ACT.Copy).then_inc(o_taken, 1)

            peer(1, 4)
            ple(1, 5)

            act.activation(tiny[:, 1, :], V8("c"), ACT.Sigmoid).then_inc(cond_sig, 1)
            root(6)
            root(7)
            m = tile0("mix_in")
            for g in range(2):
                act.activation(qaT[:, 2 * g:2 * g + 2, :], two(tile_in(m + g)), ACT.Copy).then_inc(act_took, 1)
            for g in range(2):
                act.activation(kaT[:, 2 * g:2 * g + 2, :], two(tile_in(m + 2 + g)), ACT.Copy).then_inc(act_took, 1)
            for g in range(2):
                act.activation(va[:, g, :], tile_in(m + 4 + g), ACT.Copy).then_inc(act_took, 1)
            for g in range(2):
                act.activation(qrT[:, 2 * g:2 * g + 2, :], two(tile_in(m + 6 + g)), ACT.Sigmoid).then_inc(silu_sig, 1)
            for g in range(2):
                act.activation(frT[:, 2 * g:2 * g + 2, :], two(tile_in(m + 8 + g)), ACT.Sigmoid).then_inc(act_took, 1)
            for g in range(2):
                act.activation(vr[:, g, :], tile_in(m + 10 + g), ACT.Copy).then_inc(act_took, 1)
            for g in range(2):
                act.activation(gr[:, g, :], tile_in(m + 12 + g), ACT.Sigmoid).then_inc(silu_sig, 1)
            for a in range(DIL_HEADS):
                act.wait_ge(da_in, a + 1)
                x, y = sm[:, a % 2, :], em[:, a % 2, :]
                act.activation(y[:, 0:128], x[:, 0:128], ACT.Exp, bias=dnum[:, a, 0:1])
                act.activation(y[:, 128:384], x[:, 128:384], ACT.Exp, bias=dnum[:, a, 1:2]).then_inc(da_exp, 1)
                act.wait_ge(da_turned, a + 1)
                act.activation(pmT[:, a % 2, :], psum[:, 6, 0:384], ACT.Copy).then_inc(da_copied, 1)
            act.wait_ge(lb_in, 1)
            act.activation(tiny[:, 3, 0:4], tiny[:, 2, 0:4], ACT.Sigmoid).then_inc(lb_sig, 1)
            act.wait_ge(f_ready, 1)
            act.activation(b_, f_, ACT.Ln).then_inc(logf_ready, 1)
            act.wait_ge(b_ready, 1)
            act.activation(eb, b_, ACT.Exp)
            act.activation(ke, b_, ACT.Exp, scale=-1.0)
            act.activation(decay, blast, ACT.Exp)
            act.activation(kd, kd, ACT.Exp).then_inc(eb_ready, 1)
            for a in range(REC_HEADS):
                act.wait_ge(kdt_done, a + 1)
                act.activation(kdt[:, a], two(psum[:, 4, 0:T]), ACT.Copy).then_inc(kdt_taken, 1)
            act.wait_ge(lb_in, 2)
            act.activation(hst, hst, ACT.Sqrt).then_inc(lb_sig, 1)
            root(8)
            root(9)
            act.wait_ge(gexp2_in, 1)
            act.activation(tk[:, 16:32], tk[:, 16:32], ACT.Exp).then_inc(gexp2_out, 1)
            for b in range(2):
                act.wait_ge(gather0_done, b + 1)
                act.activation(xgT[:, 4 * b:4 * b + 4, :], psum[:, 5 + b, :].rearrange("p (a b) -> p a b", a=4),
                               ACT.Copy).then_inc(gather0_taken, 1)
            m = tile0("moe")
            act.wait_ge(blocks_ready, 1)
            n = act.value_load(blocks[0:1, 0:1], min_val=E2, max_val=2 * E2)
            with act.Fori(0, n) as i:
                for s in range(4):
                    act.wait_ge(dve_took, i * 4 + TILE_NTH[m + s])
                    act.activation(sgm[:, s % 2], xg[:, s % 2], ACT.Sigmoid, scale=1.702).then_inc(sig_ready, 1)
                act.activation(SGT, tile_in(m + 4, i * BLOCK_TILES)[:, 0:T], ACT.Copy).then_inc(act_took, 1)
                for b in range(2):
                    act.activation(xgT[:, 4 * b:4 * b + 4, :],
                                   tile_in(m + 5 + b, i * BLOCK_TILES).rearrange("p (a b) -> p a b", a=4),
                                   ACT.Copy).then_inc(act_took, 1)
                for c in range(2):
                    act.activation(Y[:, c * 512:(c + 1) * 512], tile_in(m + 7 + c, i * BLOCK_TILES),
                                   ACT.Copy).then_inc(act_took, 1)
            root(10)

        @block.vector
        def _(dve):
            def tile_in(m, plus=0):
                dve.wait_ge(tile_done, plus + (m + 1))
                return psum[:, m % 3, :]

            def two(x):
                return x.rearrange("p (a b) -> p a b", a=2)

            def wide(v, n):
                return v.unsqueeze(2).to_broadcast([P, v.shape[1], n])

            def scales(i, src):
                for t in range(TT):
                    dve.tensor_tensor_reduce(out=hs[:, t, :], in0=src[:, t, :], in1=src[:, t, :], scale=1.0, scalar=0.0,
                                             op0=ALU.mult, op1=ALU.add, accum_out=ss[:, t:t + 1])
                dve.drain()
                dve.tensor_scalar(ms[:], ss[:], 1.0 / D, EPS, ALU.mult, ALU.add).then_inc(var_ready, 1)
                dve.wait_ge(std_ready, i + 1)
                dve.reciprocal(rstd[:], std[:])
                dve.drain()

            def scaled():
                for t in range(TT):
                    dve.tensor_scalar(hs[:, t, :], h[:, t, :], rstd[:, t:t + 1], None, ALU.mult).then_inc(hs_ready, 1)

            def gains(i, gain, gain2=None, shift=None):
                for b in range(4):
                    dve.wait_ge(turned, 4 * i + b + 1)
                    x = two(psum[:, 4 + b, :])
                    o = xT[:, 2 * b:2 * b + 2, :]
                    if gain2 is not None:
                        dve.tensor_tensor(xT2[:, 2 * b:2 * b + 2, :], x, wide(gain2[:, 2 * b:2 * b + 2], T), ALU.mult)
                    j = dve.tensor_tensor(o, x, wide(gain[:, 2 * b:2 * b + 2], T), ALU.mult)
                    if shift is None:
                        j.then_inc(xT_ready, 1)
                if gain2 is not None:
                    dve.drain().then_inc(xT_ready, 4)
                if shift is not None:
                    dve.drain()
                    for b in range(4):
                        o = xT[:, 2 * b:2 * b + 2, :]
                        dve.tensor_tensor(o, o, wide(shift[:, 2 * b:2 * b + 2], T), ALU.add).then_inc(xT_ready, 1)

            def low(j, n, f, it=None):
                if j % 3 == 2:
                    return
                dve.wait_ge(hi_ready, (0 if it is None else it * 48) + (j + 1))
                dve.tensor_tensor(wlo[:, j % PARTS, :], ring[:, n % RING, f * UNIT:(f + 1) * UNIT],
                                  whi[:, j % PARTS, :].bitcast(F32), ALU.subtract).then_inc(lo_ready, 1)

            dve.memset(zero[:], 0.0).then_inc(zero_ready, 1)

            dve.wait_ge(small_loaded, 32)
            nl, t0, e1, s1, s2, pl = (tiny[:, i, :] for i in (2, 0, 1, 3, 4, 5))
            dve.tensor_scalar(nl, V8("lam"), -1.0, None, ALU.mult)
            dve.drain()
            dve.tensor_tensor(t0, nl, V8("lam"), ALU.max).then_inc(spl_ready, 1)
            dve.memset(xb[:, :, 0:3], 0.0).then_inc(pads_ready, 1)
            dve.wait_ge(expl_ready, 1)
            dve.tensor_scalar(s1, e1, 2.0, None, ALU.add)
            dve.drain()
            dve.reciprocal(s2, s1)
            dve.drain()
            dve.tensor_tensor(s1, e1, s2, ALU.mult)
            dve.drain()
            dve.tensor_tensor(s2, s1, s1, ALU.mult)
            dve.memset(pl, 1.0 / 17.0)
            dve.drain()
            for k in (15, 13, 11, 9, 7, 5, 3, 1):
                dve.tensor_tensor(pl, pl, s2, ALU.mult)
                dve.drain()
                dve.tensor_scalar(pl, pl, 1.0 / k, None, ALU.add)
                dve.drain()
            dve.tensor_tensor(pl, pl, s1, ALU.mult)
            dve.tensor_scalar(nl, nl, 0.0, 4.0, ALU.max, ALU.mult)
            dve.drain()
            dve.scalar_tensor_tensor(tiny[:, 6, :], pl, 8.0, nl, ALU.mult, ALU.add).then_inc(spl_ready, 1)

            dve.wait_ge(x_loaded, 16)
            scales(0, h)
            scaled()
            gains(0, V8("norm_mix0"))
            for g in range(4):
                dve.wait_ge(act_took, 5 + g)
                for j in range(4):
                    for a in (2 * g, 2 * g + 1):
                        x, o = xb[:, a, 3 - j:3 - j + T], xc[:, a, :]
                        w = V8(f"conv{3 - j}")[:, a:a + 1]
                        if j == 0:
                            dve.tensor_scalar(o, x, w, V8("conv_b")[:, a:a + 1], ALU.mult, ALU.add)
                        else:
                            i = dve.scalar_tensor_tensor(o, x, w, o, ALU.mult, ALU.add)
                            if j == 3:
                                i.then_inc(conv_ready, 1)
                    if j < 3:
                        dve.drain()
            dve.wait_ge(act_took, TILE_NTH[tile0("a_gates") + 7])
            dve.wait_ge(conv_ready, 8)
            dve.tensor_tensor(lru[4], lru[1], xc, ALU.mult)
            dve.wait_ge(tanh_ready, 1)
            dve.tensor_scalar(lru[0], lru[2], 1.0, None, ALU.add)
            dve.drain()
            dve.reciprocal(lru[1], lru[0])
            dve.tensor_scalar(lru[5], lru[2], -1.0, 1.0, ALU.mult, ALU.add)
            dve.drain()
            dve.tensor_tensor(lru[0], lru[5], lru[1], ALU.mult)
            dve.tensor_tensor(lru[4], lru[4], lru[1], ALU.mult)
            dve.wait_ge(sqrt_ready, 1)
            dve.drain()
            dve.scalar_tensor_tensor(lru[1], lru[3], 2.0, lru[4], ALU.mult, ALU.mult)
            dve.drain()
            for a in range(KC):
                dve.tensor_tensor_scan(lru[4][:, a, :], lru[0][:, a, :], lru[1][:, a, :], 0.0, ALU.mult, ALU.add)
            dve.drain()
            dve.tensor_tensor(lru[5], lru[4], gy, ALU.mult).then_inc(gated_ready, 1)

            def add_to_residual(stage):
                m = tile0(stage)
                for g in range(4):
                    x = tile_in(m + g)
                    o = h[:, g % 2, (g // 2) * 512:(g // 2 + 1) * 512]
                    dve.tensor_tensor(o, o, x, ALU.add).then_inc(dve_took, 1)
                dve.drain()

            add_to_residual("a_out")

            def peer(l, i):
                scales(i, h)
                scaled()
                gains(i, V8(f"norm_ffn{l}"))
                dve.wait_ge(xhi_ready, l + 1)
                dve.tensor_tensor(xlo[:], xT.rearrange("p a b -> p (a b)"), xhi[:].bitcast(F32),
                                  ALU.subtract).then_inc(xlo_ready, 1)
                dve.wait_ge(act_took, TILE_NTH[tile0(f"peer_keys{l}") + 7])
                sflat = scores.rearrange("p a b c -> p (a b c)")
                cvflat = cval[:].rearrange("p a b c -> p (a b c)")
                pflat = [pick[:, r].rearrange("p a b -> p (a b)") for r in range(3)]
                iota16 = iota[:, 0:TOPK]
                wflat, cflat = work.rearrange("p a b -> p (a b)"), cand.rearrange("p a b -> p (a b)")

                def best16(vals, idx, src, spare):
                    dve.max(vals[:, 0:8], src)
                    dve.drain()
                    yield 1
                    dve.max_index(idx[:, 0:8], vals[:, 0:8], src)
                    dve.match_replace(out=spare, in_to_replace=vals[:, 0:8], in_values=src, imm_value=NEG)
                    dve.drain()
                    yield 1
                    dve.max(vals[:, 8:16], spare)
                    dve.drain()
                    dve.max_index(idx[:, 8:16], vals[:, 8:16], spare)

                def topk(at):
                    dve.tensor_copy(keys_in.rearrange("p a b -> p (a b)"), sflat[:, bass.ds(at(256), 256)])
                    dve.drain()
                    yield 1
                    for half in range(2):
                        yield from best16(sv[:, half, :], si[:, half, :], keys_in[:, half, :], wflat[:, half * P:(half + 1) * P])
                    dve.drain()
                    yield 1
                    dve.tensor_copy(sif[:], si[:])
                    dve.tensor_tensor(cand, sv[:, 0, :].unsqueeze(2).to_broadcast([P, TOPK, TOPK]),
                                      sv[:, 1, :].unsqueeze(1).to_broadcast([P, TOPK, TOPK]), ALU.add)
                    dve.drain()
                    yield 1
                    yield from best16(cv, ci, cflat, wflat)
                    dve.drain()
                    yield 1
                    dve.tensor_copy(cvflat[:, bass.ds(at(TOPK), TOPK)], cv[:])
                    dve.tensor_single_scalar(cab[:, 0, :], ci[:], 4, ALU.logical_shift_right)
                    dve.tensor_single_scalar(cab[:, 1, :], ci[:], 15, ALU.bitwise_and)
                    dve.drain()
                    yield 1
                    dve.tensor_copy(cabf[:], cab[:])
                    dve.drain()
                    yield 1
                    for half in range(2):
                        w = work if half else cand
                        dve.tensor_tensor(w, iota16.unsqueeze(1).to_broadcast([P, TOPK, TOPK]),
                                          cabf[:, half, :].unsqueeze(2).to_broadcast([P, TOPK, TOPK]), ALU.is_equal)
                    dve.drain()
                    yield 1
                    for half in range(2):
                        w = work if half else cand
                        dve.tensor_tensor(w, w, sif[:, half, :].unsqueeze(1).to_broadcast([P, TOPK, TOPK]),
                                          ALU.mult)
                    dve.drain()
                    yield 1
                    for half in range(2):
                        w = work if half else cand
                        dve.tensor_reduce(pflat[half][:, bass.ds(at(TOPK), TOPK)], w, AX.X, ALU.add)
                    dve.drain()
                    yield 1
                def topk_end():
                    for t in range(TT):
                        dve.tensor_tensor(pick[:, 2, t].rearrange("p (a b) -> p a b", a=PH), cval[:, t],
                                          cval[:, t, :, 0:1].to_broadcast([P, PH, TOPK]), ALU.subtract)
                    dve.drain()
                    dve.tensor_copy(cval[:].rearrange("p a b c -> p (a b c)"), pflat[2]).then_inc(gexp_in, 1)

                n0, u0 = FIRST[f"peer_u{l}"], FIRST_UNIT[f"peer_u{l}"]
                for j in range(PARTS):
                    low(u0 + j, n0, j)
                with dve.Fori(0, 4) as it:
                    for r in range(4):
                        steps = topk(lambda n: it * (4 * n) + r * n)
                        for q in range(12):
                            j = 12 * r + q + PARTS
                            low(u0 + j, n0 + j // UNITS, j % UNITS, it)
                            for _ in range(2 if q < 11 else 99):
                                if next(steps, 0) == 0:
                                    break
                dve.drain().then_inc(topk_done, 1)
                for j in range(192 + PARTS, 256 + PARTS - 1):
                    if j == 192 + 8:
                        topk_end()
                    low(u0 + j, n0 + j // UNITS, j % UNITS)
                dve.wait_ge(gexp_out, l + 1)
                sums = tiny[:, 7:9, :]
                for t in range(TT):
                    dve.tensor_reduce(sums[:, t, :], cval[:, t], AX.X, ALU.add)
                dve.drain()
                dve.reciprocal(sums, sums)
                dve.drain()
                for t in range(TT):
                    dve.tensor_tensor(pick[:, 2, t].rearrange("p (a b) -> p a b", a=PH), cval[:, t],
                                      sums[:, t, :].unsqueeze(2).to_broadcast([P, PH, TOPK]), ALU.mult)
                dve.drain().then_inc(pick_ready, 1)
                dve.wait_ge(pick_turned, l + 1)
                dve.tensor_copy(pickT[:, 0:2, :], two(psum[:, 4, :]))
                dve.tensor_copy(pickT[:, 2, :], psum[:, 5, 0:T])
                dve.drain().then_inc(pickT_ready, 1)
                dve.wait_ge(act_took, TILE_NTH[tile0(f"peer_v{l}") - 1])
                dve.wait_ge(tile_done, tile0(f"peer_v{l}"))
                kflat = scratch

                def one_hot(g, at):
                    for k in range(4):
                        i = dve.tensor_scalar(hot2(g % 2, k), iota, kflat[:, bass.ds(at + (T + k), 1)],
                                              kflat[:, bass.ds(at + (2 * T + k), 1)], ALU.is_equal, ALU.mult)
                    i.then_inc(hot_ready, 1)

                def gate(g, at, n):
                    dve.wait_ge(wmat_done, n)
                    x = acts[:, :, bass.ds(at, 4)]
                    dve.tensor_tensor(x, x, psum[:, 4 + g % 4, :].rearrange("p (t i) -> p i t", t=4),
                                      ALU.mult).then_inc(gated_acts, 1)

                one_hot(0, 0)
                with dve.Fori(0, 15) as it:
                    for g in range(4):
                        one_hot(g + 1, it * 16 + 4 * (g + 1))
                        gate(g, it * 16 + 4 * g, it * 4 + (64 * l + g + 1))
                for g in range(60, 64):
                    if g < 63:
                        one_hot(g + 1, 4 * (g + 1))
                    gate(g, 4 * g, 64 * l + g + 1)
                n0, u0 = FIRST[f"peer_v{l}"], FIRST_UNIT[f"peer_v{l}"]
                aflat = acts.rearrange("p a b -> p (a b)")

                def stage(s, at, plus=0):
                    dve.wait_ge(vhi_ready, plus + (32 * l + s + 1))
                    dve.tensor_tensor(vlo[:, s % 2, :], aflat[:, bass.ds(at, D)], vhi[:, s % 2, :].bitcast(F32),
                                      ALU.subtract).then_inc(vlo_ready, 1)

                def v_slots(slots, s0, it=None):
                    for s in range(s0, s0 + slots):
                        for q in range(UNITS):
                            j = UNITS * s + q + PARTS
                            if j < 256:
                                low(u0 + j, n0 + j // UNITS, j % UNITS, it)
                            if q == 3 and s < 31:
                                if it is None:
                                    stage(s + 1, (s + 1) * D)
                                else:
                                    stage(s + 1, it * (6 * D) + (s + 1) * D, it * 6)

                stage(0, 0)
                low(u0 + PARTS - 1, n0, PARTS - 1)
                with dve.Fori(0, 5) as it:
                    v_slots(6, 0, it)
                v_slots(2, 30)
                dve.wait_ge(tile_done, ENDS[FIRST[f"peer_v{l}"] + 31])
                for t in range(TT):
                    for c in range(2):
                        o = h[:, t, c * 512:(c + 1) * 512]
                        dve.tensor_tensor(o, o, psum[:, 4 + 2 * t + c, :], ALU.add)
                dve.drain()

            def ple(l, i):
                scales(i, h)
                scaled()
                gains(i, V8(f"norm_ple{l}"))
                m = tile0(f"ple_proj{l}")
                dve.wait_ge(act_took, TILE_NTH[m - 1])
                for g in range(4):
                    c = slice((g % 2) * 512, (g % 2 + 1) * 512)
                    dve.tensor_tensor(ple_t[:, g // 2, c], tile_in(m + g), gate_sb[:, g // 2, c],
                                      ALU.mult).then_inc(dve_took, 1)
                dve.drain()
                dve.tensor_tensor(h[:], h[:], ple_t, ALU.add)
                dve.drain()

            peer(0, 1)
            ple(0, 2)

            scales(3, h)
            scaled()
            gains(3, V8("kv_norm"), gain2=V8("norm_mix1"))
            dve.wait_ge(late_loaded, 16)
            mask = late[:, C_MASK:C_MASK + 384]
            for a in range(HEADS):
                z = psum[:, 4 + a % 4, 0:384]
                dve.wait_ge(zlog_ready, a + 1)
                pos = za[:, 2, a % 2, :]
                dve.tensor_scalar(pos, z, SC, 0.0, ALU.mult, ALU.max)
                dve.drain()
                dve.tensor_tensor(pos, pos, zl[:, a % 2, :], ALU.add)
                dve.drain()
                dve.scalar_tensor_tensor(w_sb[:, a, :], z, SC, pos, ALU.mult, ALU.subtract)
                dve.tensor_tensor(lm[:, a, :], pos, mask, ALU.mult)
                dve.drain().then_inc(lm_ready, 1)

            def masked(a):
                dve.wait_ge(aexp_out, a + 1)
                dve.tensor_tensor(w_sb[:, a, :], w_sb[:, a, :], mask, ALU.mult).then_inc(a_ready, 1)

            for a in range(HEADS):
                dve.wait_ge(suffix_done, a + 1)
                dve.tensor_tensor(w_sb[:, a, :], w_sb[:, a, :], psum[:, 4 + a % 4, 0:384],
                                  ALU.subtract).then_inc(aexp_in, 1)
                if a:
                    masked(a - 1)
            masked(HEADS - 1)
            add_to_residual("bo")

            peer(1, 4)
            ple(1, 5)

            def spread(i, vec, row=row):
                for k in range(KC):
                    j = dve.tensor_scalar(diag[:, k, :], ident, vec[:, k:k + 1], None, ALU.mult)
                j.then_inc(diag_ready, 1)
                dve.wait_ge(row_done, i + 1)
                dve.tensor_copy(row.rearrange("p (a b) -> p a b", a=2), psum[:, 4:6, :])
                dve.drain()

            dve.wait_ge(late_loaded, 32)
            spread(0, V8("final_norm"))
            scales(6, h)
            for t in range(TT):
                dve.scalar_tensor_tensor(h[:, t, :], h[:, t, :], rstd[:, t:t + 1], row, ALU.mult, ALU.mult)
            dve.wait_ge(cond_sig, 1)
            dve.tensor_tensor(tiny[:, 0, :], tiny[:, 1, :], V8("c"), ALU.mult).then_inc(cond_ready, 1)
            m = tile0("ada")
            avec = vecs[:, V["ada0"]:V["ada0"] + 6, :].rearrange("p a b -> p (a b)")
            for g in range(12):
                x = tile_in(m + g)
                dve.tensor_copy(mod_row[0:1, g * 512:(g + 1) * 512], x[0:1, :]).then_inc(dve_took, 1)
            dve.wait_ge(mod_turned, 1)
            dve.tensor_tensor(modv[:], psum[:, 3, 0:48], avec, ALU.add)
            dve.drain()
            shift_m, scale_m, gate_m, shift_f, scale_f, gate_f = (modv[:, 8 * i:8 * i + 8] for i in range(6))
            gm, gf, rm, rf = (tiny[:, i, :] for i in (9, 10, 11, 12))
            dve.scalar_tensor_tensor(gm, scale_m, 1.0, V8("g_pre_mix"), ALU.add, ALU.mult)
            dve.scalar_tensor_tensor(gf, scale_f, 1.0, V8("g_pre_ffn"), ALU.add, ALU.mult)
            dve.tensor_tensor(rm, gate_m, V8("g_post_mix"), ALU.mult)
            dve.tensor_tensor(rf, gate_f, V8("g_post_ffn"), ALU.mult)
            dve.drain()
            scales(7, h)
            scaled()
            gains(6, gm, shift=shift_m)
            m = tile0("mix_in")
            for g in range(2):
                dve.wait_ge(silu_sig, g + 1)
                o = qrT[:, 2 * g:2 * g + 2, :]
                dve.tensor_tensor(o, o, two(psum[:, (m + 6 + g) % 3, :]), ALU.mult).then_inc(dve_took, 1)
            for g in range(2):
                dve.wait_ge(silu_sig, g + 3)
                o = gr[:, g, :]
                dve.tensor_tensor(o, o, psum[:, (m + 12 + g) % 3, :], ALU.mult).then_inc(dve_took, 1)

            neg, cnt = late[:, C_NEG:C_NEG + 384], late[:, C_CNT:C_CNT + 384]
            for a in range(DIL_HEADS):
                dve.wait_ge(da_done, a + 1)
                x = sm[:, a % 2, :]
                y = em[:, a % 2, :]
                dve.scalar_tensor_tensor(x, psum[:, 4 + a % 2, 0:384], SC, neg, ALU.mult, ALU.add)
                dve.drain()
                dve.tensor_reduce(dnum[:, a, 0:1], x[:, 0:128], AX.X, ALU.max, negate=True)
                dve.tensor_reduce(dnum[:, a, 1:2], x[:, 128:384], AX.X, ALU.max, negate=True)
                dve.drain().then_inc(da_in, 1)
                dve.wait_ge(da_exp, a + 1)
                for t, c in ((0, slice(0, 128)), (1, slice(128, 384))):
                    dve.tensor_tensor_reduce(out=y[:, c], in0=y[:, c], in1=cnt[:, c], scale=1.0, scalar=0.0,
                                             op0=ALU.mult, op1=ALU.add, accum_out=dnum[:, a, 2 + t:3 + t])
                dve.drain().then_inc(da_p, 1)
                dve.reciprocal(dnum[:, a, 2:4], dnum[:, a, 2:4])
                dve.drain()
                dve.wait_ge(da_o, a + 1)
                dve.tensor_tensor(ylow[:, :, a * 64:a * 64 + 64], two(psum[:, 7, 0:128]), wide(dnum[:, a, 2:4], 64),
                                  ALU.mult).then_inc(da_taken, 1)

            dve.tensor_tensor(tiny[:, 2, 0:4], V8("lb")[:, 0:4], V8("lb")[:, 4:8], ALU.subtract).then_inc(lb_in, 1)
            dve.wait_ge(lb_sig, 1)
            dve.tensor_scalar(tiny[:, 4, 0:4], tiny[:, 3, 0:4], -1.0, 1.0, ALU.mult, ALU.add)
            dve.drain()
            dve.wait_ge(act_took, TILE_NTH[tile0("mix_in") + 11])
            for a in range(REC_HEADS):
                i = dve.tensor_scalar(f_[:, a, :], frT[:, a, :], tiny[:, 4, a:a + 1], tiny[:, 3, a:a + 1],
                                      ALU.mult, ALU.add)
            i.then_inc(f_ready, 1)
            dve.wait_ge(logf_ready, 1)
            reset = late[:, C_RESET:C_RESET + T]
            for a in range(REC_HEADS):
                dve.tensor_tensor_scan(frT[:, a, :], reset, b_[:, a, :], 0.0, ALU.mult, ALU.add)
            dve.drain()
            by_chunk = [v.rearrange("p a (n c) -> p a n c", c=CHUNK) for v in (frT, kd)]
            dve.tensor_copy(b_, frT)
            for a in range(REC_HEADS):
                dve.tensor_copy(blast[:, a, :].unsqueeze(2), by_chunk[0][:, a, :, CHUNK - 1:CHUNK])
            dve.drain()
            for a in range(REC_HEADS):
                dve.tensor_tensor(by_chunk[1][:, a], blast[:, a, :].unsqueeze(2).to_broadcast([P, 8, CHUNK]),
                                  by_chunk[0][:, a], ALU.subtract)
            dve.drain().then_inc(b_ready, 1)
            dve.tensor_scalar(f_, f_, -1.0, 1.0, ALU.mult, ALU.add)
            dve.drain()
            dve.wait_ge(eb_ready, 1)
            for a in range(REC_HEADS):
                dve.tensor_tensor(qe[:, a, :], qrT[:, a, :], eb[:, a, :], ALU.mult).then_inc(kd_ready, 1)
                dve.tensor_tensor(ke[:, a, :], ke[:, a, :], f_[:, a, :], ALU.mult).then_inc(kd_ready, 1)
                dve.tensor_tensor(kd[:, a, :], kd[:, a, :], f_[:, a, :], ALU.mult).then_inc(kd_ready, 1)
            dve.memset(am, 0.0)
            dve.drain()
            rmask = late[:, C_REC:C_REC + P].bitcast(I32)
            for a in range(REC_HEADS):
                dve.wait_ge(am_done, a + 1)
                for t in range(TT):
                    dve.copy_predicated(am[:, a, t, :], rmask, psum[:, 5, t * P:(t + 1) * P]).then_inc(am_taken, 1)
            for c in range(7):
                dve.wait_ge(delta_done, c + 1)
                for a in range(REC_HEADS):
                    x = psum[:, 4 + c % 2, a * P:(a + 1) * P]
                    o = states[:, (c + 1) % 4, a, :]
                    if c == 0:
                        dve.tensor_copy(o, x).then_inc(state_ready, 1)
                    else:
                        if c == 4:
                            dve.wait_ge(ro_done, 1)
                        dve.wait_ge(state_ready, 4 * (c - 1) + a + 1)
                        dve.scalar_tensor_tensor(o, states[:, c % 4, a, :], decay[:, a, c:c + 1], x, ALU.mult,
                                                 ALU.add).then_inc(state_ready, 1)
            dve.wait_ge(ro_done, 2)
            for t in range(TT):
                dve.tensor_copy(ylow[:, t, 512:1024], psum[:, 6 + t, :])
            dve.drain()
            dve.tensor_tensor(sq, ylow, ylow, ALU.mult)
            dve.drain()
            for t in range(TT):
                dve.tensor_reduce(hst[:, t * 12:t * 12 + 8], sq[:, t, 0:512].rearrange("p (a b) -> p a b", a=8),
                                  AX.X, ALU.add)
                dve.tensor_reduce(hst[:, t * 12 + 8:t * 12 + 12], sq[:, t, 512:1024].rearrange("p (a b) -> p a b", a=4),
                                  AX.X, ALU.add)
            dve.drain()
            for t in range(TT):
                for a, b, n in ((0, 8, 64), (8, 12, 128)):
                    o = hst[:, t * 12 + a:t * 12 + b]
                    dve.tensor_scalar(o, o, 1.0 / n, EPS, ALU.mult, ALU.add)
            dve.drain().then_inc(lb_in, 1)
            dve.wait_ge(lb_sig, 2)
            dve.reciprocal(hst, hst)
            dve.drain()
            for t in range(TT):
                for a, b, c0, n in ((0, 8, 0, 64), (8, 12, 512, 128)):
                    o = ylow[:, t, c0:c0 + 512].rearrange("p (a b) -> p a b", b=n)
                    dve.tensor_tensor(o, o, wide(hst[:, t * 12 + a:t * 12 + b], n), ALU.mult)
            dve.drain()
            for t in range(TT):
                o = ylow[:, t, 512:1024]
                dve.tensor_tensor(o, o, gr[:, t, :], ALU.mult)
            dve.drain().then_inc(hs_ready, 2)
            gains(7, V8("mix_norm"))
            m = tile0("mix_out")
            for g in range(4):
                dve.tensor_copy(ysb[:, g % 2, (g // 2) * 512:(g // 2 + 1) * 512], tile_in(m + g)).then_inc(dve_took, 1)
            dve.drain()
            spread(1, rm)
            scales(8, ysb)

            def add_row_scaled(src, out):
                for t in range(TT):
                    dve.scalar_tensor_tensor(src[:, t, :], src[:, t, :], rstd[:, t:t + 1], row, ALU.mult, ALU.mult)
                dve.drain()
                for t in range(TT):
                    i = dve.tensor_tensor(out[:, t, :], h[:, t, :], src[:, t, :], ALU.add)
                    if out is hs:
                        i.then_inc(y_ready, 1)
                dve.drain()

            add_row_scaled(ysb, h)
            scales(9, h)
            scaled()
            gains(8, gf, shift=shift_f)
            spread(2, gf)
            spread(3, shift_f, row2)
            for t in range(TT):
                dve.tensor_tensor(hs[:, t, :], hs[:, t, :], row, ALU.mult)
            dve.drain()
            for t in range(TT):
                dve.tensor_tensor(hs[:, t, :], hs[:, t, :], row2, ALU.add)
            dve.drain()

            dve.wait_ge(logits_done, 1)
            dve.tensor_copy(logit, psum[:, 3, 0:2 * E2].rearrange("p (a b) -> p a b", a=2))
            dve.drain()
            for t in range(TT):
                dve.max(tk[:, 8 * t:8 * t + 8], logit[:, t, :])
            dve.drain()
            for t in range(TT):
                dve.max_index(tki[:, 8 * t:8 * t + 8], tk[:, 8 * t:8 * t + 8], logit[:, t, :])
                dve.tensor_scalar(tk[:, 16 + 8 * t:24 + 8 * t], tk[:, 8 * t:8 * t + 8], tk[:, 8 * t:8 * t + 1], None,
                                  ALU.subtract)
            dve.drain().then_inc(gexp2_in, 1)
            dve.tensor_copy(tk[:, 32:48], tki)
            dve.wait_ge(gexp2_out, 1)
            for t in range(TT):
                dve.tensor_reduce(tk[:, 48 + t:49 + t], tk[:, 16 + 8 * t:20 + 8 * t], AX.X, ALU.add)
            dve.drain()
            dve.reciprocal(tk[:, 50:52], tk[:, 48:50])
            dve.drain()
            for t in range(TT):
                dve.tensor_scalar(tk[:, 16 + 8 * t:20 + 8 * t], tk[:, 16 + 8 * t:20 + 8 * t], tk[:, 50 + t:51 + t], None,
                                  ALU.mult)
            dve.memset(G, 0.0)
            dve.memset(member, 0.0)
            dve.memset(Y, 0.0)
            dve.memset(SGT, 0.0)
            dve.drain()
            i32 = late[:, C_IOTA32:C_IOTA32 + E2]
            for k in range(4):
                for t in range(TT):
                    dve.tensor_scalar(logit[:, t, :], i32, tk[:, 32 + 8 * t + k:33 + 8 * t + k], None, ALU.is_equal)
                dve.drain()
                for t in range(TT):
                    dve.tensor_tensor(member[:, t, :], member[:, t, :], logit[:, t, :], ALU.add)
                    dve.scalar_tensor_tensor(G[:, t, :], logit[:, t, :], tk[:, 16 + 8 * t + k:17 + 8 * t + k],
                                             G[:, t, :], ALU.mult, ALU.add)
                dve.drain()
            dve.drain().then_inc(member_ready, 1)
            dve.wait_ge(ranks_done, 1)
            ranks = psum[:, 3, 0:2 * E2].rearrange("p (a b) -> p a b", a=2)
            dve.memset(rank[:, :, 2 * E2:66], -1.0)
            dve.memset(G2[:, :, 2 * E2:66], 0.0)
            for t in range(TT):
                dve.scalar_tensor_tensor(rank[:, t, 0:E2], ranks[:, t, :], 1.0, member[:, t, :], ALU.add, ALU.mult)
                dve.tensor_copy(G2[:, t, 0:E2], G[:, t, :])
                dve.tensor_copy(G2[:, t, E2:2 * E2], G[:, t, :])
            dve.tensor_reduce(most[:, 0:1], psum[:, 3, 2 * E2:3 * E2], AX.X, ALU.max)
            dve.drain()
            for t in range(TT):
                dve.tensor_scalar(rank[:, t, 0:E2], rank[:, t, 0:E2], -1.0, None, ALU.add)
            dve.tensor_scalar(most[:, 1:2], most[:, 0:1], P + 0.5, float(E2), ALU.is_gt, ALU.mult)
            dve.drain()
            for t in range(TT):
                dve.tensor_scalar(rank[:, t, E2:2 * E2], rank[:, t, 0:E2], -float(P), None, ALU.add)
            dve.tensor_scalar(most[:, 2:3], most[:, 1:2], float(E2), None, ALU.add)
            dve.drain()
            dve.tensor_copy(blocks, most[:, 2:3])
            for t in range(TT):
                dve.tensor_scalar(S[:, t, :], iota, rank[:, t, 0:1], None, ALU.is_equal)
            dve.wait_ge(gT_done, 1)
            dve.tensor_copy(gT[0:E2, :], psum[0:E2, 4, 0:T])
            dve.drain().then_inc(first_S, 1)
            dve.drain().then_inc(blocks_ready, 1)

            m = tile0("moe")
            rflat, gflat = (v.rearrange("p a b -> p (a b)") for v in (rank, G2))
            bflat = bgu.rearrange("p a b -> p (a b)")
            n = dve.value_load(blocks[0:1, 0:1], min_val=E2, max_val=2 * E2)
            with dve.Fori(0, n) as i:
                for s in range(4):
                    x = tile_in(m + s, i * BLOCK_TILES)
                    for f in range(2):
                        dve.tensor_scalar(xg[:, s % 2, f, :], x[:, f * P:(f + 1) * P],
                                          bflat[:, bass.ds(i * 16 + (2 * s + f), 1)], 7.0, ALU.add, ALU.min)
                    for f in range(2):
                        j = dve.tensor_scalar(lin[:, s % 2, f, :], x[:, (2 + f) * P:(3 + f) * P],
                                              bflat[:, bass.ds(i * 16 + (8 + 2 * s + f), 1)], 7.0, ALU.add, ALU.min)
                    j.then_inc(dve_took, 1)
                    dve.drain()
                    if s == 0:
                        for t in range(TT):
                            dve.tensor_scalar(S[:, t, :], iota, rflat[:, bass.ds(i + (t * 66 + 1), 1)], None, ALU.is_equal)
                            dve.tensor_scalar(SG[:, t, :], iota, rflat[:, bass.ds(i + t * 66, 1)],
                                              gflat[:, bass.ds(i + t * 66, 1)], ALU.is_equal, ALU.mult)
                        dve.drain().then_inc(S_ready, 1)
                    dve.tensor_scalar(lin[:, s % 2], lin[:, s % 2], -7.0, 1.0, ALU.max, ALU.add)
                    dve.drain()
                    dve.tensor_tensor(lin[:, s % 2], lin[:, s % 2], xg[:, s % 2], ALU.mult)
                    dve.drain()
                    dve.wait_ge(sig_ready, i * 4 + (s + 1))
                    dve.tensor_tensor(actT[:, 2 * s:2 * s + 2, :], lin[:, s % 2], sgm[:, s % 2], ALU.mult).then_inc(act_ready, 1)
            dve.wait_ge(moe_done, 1)
            for t in range(TT):
                dve.tensor_copy(acc[:, t, :].rearrange("p (a b) -> p a b", a=2), psum[:, 4 + 2 * t:6 + 2 * t, :])
            dve.drain()
            spread(4, rf)
            scales(10, acc)
            add_row_scaled(acc, hs)

        @block.gpsimd
        def _(pool):
            def low(j, n, f, it=None):
                if j % 3 != 2:
                    return
                pool.wait_ge(hi_ready, (0 if it is None else it * 48) + (j + 1))
                pool.tensor_tensor(wlo[:, j % PARTS, :], ring[:, n % RING, f * UNIT:(f + 1) * UNIT],
                                   whi[:, j % PARTS, :].bitcast(F32), ALU.subtract).then_inc(pool_lo_ready, 1)

            def lows(stage, start, end):
                n0, u0 = FIRST[stage], FIRST_UNIT[stage]
                rounds = (end - start) // 48
                with pool.Fori(0, rounds) as it:
                    for j in range(start, start + 48):
                        low(u0 + j, n0 + j // UNITS, j % UNITS, it)
                for j in range(start + 48 * rounds, end):
                    low(u0 + j, n0 + j // UNITS, j % UNITS)

            for l in range(2):
                lows(f"peer_u{l}", 0, 256 + PARTS - 1)
                pool.wait_ge(pickT_ready, l + 1)
                pool.wait_ge(tile_done, tile0(f"peer_v{l}"))

                def distances(b, at):
                    pool.tensor_tensor(away[:, b], iota.unsqueeze(1).to_broadcast([P, 4, P]),
                                       scratch[:, bass.ds(at, 4)].unsqueeze(2).to_broadcast([P, 4, P]),
                                       ALU.subtract).then_inc(away_ready, 1)

                distances(0, 0)
                distances(1, 4)
                with pool.Fori(0, 31) as it:
                    for b in range(2):
                        pool.wait_ge(hot1_ready, it * 2 + (64 * l + b + 1))
                        distances(b, it * 8 + (4 * b + 8))
                lows(f"peer_v{l}", PARTS - 1, 256)
            pool.wait_ge(hs_ready, 18)
            for i in range(2):
                pool.dma_start(bgu[:, i * E2:(i + 1) * E2], d["bgu"]).then_inc(moe_loaded, 16)
            pool.dma_start(bdn[0:E2, :], d["bdn"]).then_inc(moe_loaded, 16)
            pool.dma_start(wr, d["wr"]).then_inc(moe_loaded, 16)
            pool.dma_start(br[0:1, :], d["br"]).then_inc(moe_loaded, 16)


def _columns(w, width=512):
    k, n = w.shape
    return np.ascontiguousarray(
        w.reshape(k // P, P, n // width, width).transpose(2, 1, 0, 3)).reshape(n // width, P, k // P * width)


def _vec(v):
    return v.reshape(-1, 8, P).transpose(2, 0, 1)


def kernel(**inputs):
    import concourse.bacc as bacc
    from concourse.bass_utils import run_bass_kernel_spmd as run

    a = {k: np.ascontiguousarray(v) for k, v in inputs.items()}
    out = {"x": a["x"]}
    out["small"], out["late"] = constant_tables()
    pairs = [a["norm_mix"], a["kv_norm"][None], a["norm_ffn"], a["norm_ple"], a["final_norm"][None], a["a_conv_w"][0],
             a["a_conv_b"], a["a_b_r"], a["a_b_i"], a["a_lambda"], a["g_pre_mix_2"], a["g_post_mix_2"],
             a["g_pre_ffn_2"], a["g_post_ffn_2"], np.concatenate([a["attn_norm_w_2"], a["hgrn_norm_w_2"]], 1),
             a["c_2"], a["hgrn_lb_2"].reshape(1, D), a["b_ada_2"].reshape(6, D)]
    out["vecs"] = np.ascontiguousarray(_vec(np.concatenate(pairs, 0)))
    out["a_in"] = _columns(a["a_w_in"][0])
    out["a_gates"] = np.ascontiguousarray(
        np.concatenate([a["a_w_r"][0], a["a_w_i"][0]], 0).transpose(1, 0, 2)).reshape(P, 16 * P)
    out["a_out"] = _columns(a["a_w_out"][0])
    out["peer_wq"] = np.stack([_columns(w) for w in a["peer_w_q"]])
    out["keys"] = np.ascontiguousarray(
        a["peer_sub_keys"].reshape(2, 16, NK, P).transpose(0, 3, 1, 2)).reshape(2, P, 16 * NK)
    out["peer_u"] = np.ascontiguousarray(
        a["peer_u"].reshape(2, P, 32, 4, KC, P).transpose(0, 2, 5, 3, 4, 1)).reshape(2, 32, P, SLOT)
    out["peer_v"] = np.ascontiguousarray(
        a["peer_v"].reshape(2, P, 32, SLOT).transpose(0, 2, 1, 3))
    out["ple_gate"] = np.stack([_columns(w) for w in a["ple_w_gate"]])
    out["ple_proj"] = np.ascontiguousarray(
        a["ple_w_proj"].reshape(2, 2, P, D).transpose(0, 2, 1, 3)).reshape(2, P, 2 * D)
    out["pT"] = np.ascontiguousarray(a["p"].reshape(2, T, 2, P).transpose(0, 3, 2, 1))
    out["kv"] = _columns(a["w_kv"])
    out["bq"] = _columns(a["b_w_q"][0])
    out["bo"] = _columns(a["b_w_o"][0])
    out["ada"] = _columns(a["w_ada_2"][0])
    out["mix_in"] = _columns(a["w_in_2"][0])
    out["mix_out"] = _columns(a["w_out_2"][0])
    moe = np.empty((E2, 6, P, SLOT), np.float32)
    moe[:, 0:4] = a["w_gu_2"][0].reshape(E2, KC, P, 2, 4, 2, P).transpose(0, 4, 2, 3, 5, 1, 6).reshape(E2, 4, P, SLOT)
    moe[:, 4:6] = a["w_down_2"][0].reshape(E2, KC, P, 2, 512).transpose(0, 3, 2, 1, 4).reshape(E2, 2, P, SLOT)
    out["moe"] = moe
    out["bgu"] = np.ascontiguousarray(a["b_gu_2"][0].reshape(E2, 16, P).transpose(2, 0, 1))
    out["bdn"] = a["b_down_2"][0]
    out["wr"] = np.ascontiguousarray(a["w_router_2"][0].reshape(KC, P, E2).transpose(1, 0, 2))
    out["br"] = a["b_router_2"]

    nc = bacc.Bacc("TRN2", target_bir_lowering=False, num_devices=1)
    d = {k: nc.dram_tensor(f"in_{k}", v.shape, F32, kind="ExternalInput").ap() for k, v in out.items()}
    d["out"] = nc.dram_tensor("out_0", (1, T, D), F32, kind="ExternalOutput").ap()
    build(nc, d)
    r = run(nc, [{f"in_{k}": v for k, v in out.items()}], core_ids=[0])
    return r.results[0]["out_0"]
```
